# Optimizing a Trainium2 kernel written in Bass

```python
import jax, jax.numpy as jnp
from jax import lax
import numpy as np

D_MODEL = 1024
BATCH = 1
SEQ = 512
DEPTH = 2
DEC_BATCH = 8
DEC_SEQ = 16
PAST_LEN = 256

CHUNK = 64
Q_BLOCK = 128
D_PLE = 256
N_HEADS_A = 8
QK_NOPE = 64
QK_ROPE = 32
V_HEAD = 64
KV_LORA = 128
Q_LORA = 256
WIDTH_A = N_HEADS_A * V_HEAD
CONV_CH = D_MODEL // 2
CONV_W = 31
CONV_STATE = CONV_W - 1
D_MIX = WIDTH_A + CONV_CH
D_IN = Q_LORA + KV_LORA + QK_ROPE + WIDTH_A + 2 * CONV_CH + CONV_CH
ROPE_THETA = 10000.0
ATTN_SCALE = (QK_NOPE + QK_ROPE) ** -0.5
EPS = 1e-6
NEG_INF = -1e30

kernel_name = "hymba_mla_conformer_stream_step"

def rmsnorm(x, g):
    xf = x.astype(jnp.float32)
    y = xf * lax.rsqrt(jnp.mean(xf * xf, axis=-1, keepdims=True) + EPS)
    return (y * g.astype(jnp.float32)).astype(x.dtype)

def layernorm(x, g, b):
    xf = x.astype(jnp.float32)
    mu = jnp.mean(xf, axis=-1, keepdims=True)
    xc = xf - mu
    var = jnp.mean(xc * xc, axis=-1, keepdims=True)
    y = xc * lax.rsqrt(var + EPS) * g.astype(jnp.float32) + b.astype(jnp.float32)
    return y.astype(x.dtype)

def rope(x, pos):
    half = QK_ROPE // 2
    inv = ROPE_THETA ** (-jnp.arange(half, dtype=jnp.float32) / half)
    ang = pos.astype(jnp.float32)[:, None] * inv[None, :]
    cos = jnp.cos(ang)[None, :, None, :]
    sin = jnp.sin(ang)[None, :, None, :]
    x1 = x[..., :half].astype(jnp.float32)
    x2 = x[..., half:].astype(jnp.float32)
    return jnp.concatenate([x1 * cos - x2 * sin, x1 * sin + x2 * cos], axis=-1).astype(x.dtype)

def mla_attend(q_lat, q_rope, ckv, krope, mask):
    s = (jnp.einsum('bthr,bsr->bhts', q_lat, ckv)
         + jnp.einsum('bthe,bse->bhts', q_rope, krope)).astype(jnp.float32) * ATTN_SCALE
    if mask is not None:
        s = jnp.where(mask[None, None], s, NEG_INF)
    p = jax.nn.softmax(s, axis=-1).astype(ckv.dtype)
    return jnp.einsum('bhts,bsr->bthr', p, ckv)

def prompt_attention(q_lat, q_rope, ckv, krope):
    b, t = q_lat.shape[0], q_lat.shape[1]
    nb = t // Q_BLOCK
    ql = q_lat.reshape(b, nb, Q_BLOCK, N_HEADS_A, KV_LORA).transpose(1, 0, 2, 3, 4)
    qr = q_rope.reshape(b, nb, Q_BLOCK, N_HEADS_A, QK_ROPE).transpose(1, 0, 2, 3, 4)
    k_chunk = jnp.arange(t) // CHUNK

    def block(args):
        ql_b, qr_b, i = args
        q_chunk = (i * Q_BLOCK + jnp.arange(Q_BLOCK)) // CHUNK
        mask = k_chunk[None, :] <= q_chunk[:, None]
        return mla_attend(ql_b, qr_b, ckv, krope, mask)

    o = lax.map(block, (ql, qr, jnp.arange(nb)))
    return o.transpose(1, 0, 2, 3, 4).reshape(b, t, N_HEADS_A, KV_LORA)

def causal_dwconv(u_pad, w, bias):
    y = lax.conv_general_dilated(u_pad, w[:, None, :], window_strides=(1,), padding='VALID',
                                 dimension_numbers=('NWC', 'WIO', 'NWC'),
                                 feature_group_count=CONV_CH)
    return y + bias

def mixer_layer(h, p, pos, ckv_past, krope_past, conv_past,
                ln_in, w_in, ln_q, w_q_b, ln_kv, w_kv_b, conv_w, conv_b,
                ln_conv_g, ln_conv_b, ln_out_a, ln_out_c, w_out, w_pe, ln_pg, w_pg):
    b, t = h.shape[0], h.shape[1]
    z = rmsnorm(h, ln_in) @ w_in
    i1 = Q_LORA
    i2 = i1 + KV_LORA
    i3 = i2 + QK_ROPE
    i4 = i3 + WIDTH_A
    i5 = i4 + CONV_CH
    i6 = i5 + CONV_CH
    c_q, c_kv, k_r, g_a, u_val, u_gate, g_c = jnp.split(z, [i1, i2, i3, i4, i5, i6], axis=-1)

    q = (rmsnorm(c_q, ln_q) @ w_q_b).reshape(b, t, N_HEADS_A, QK_NOPE + QK_ROPE)
    q_nope = q[..., :QK_NOPE]
    q_rope = rope(q[..., QK_NOPE:], pos)
    ckv_new = rmsnorm(c_kv, ln_kv)
    kr_new = rope(k_r[:, :, None, :], pos)[:, :, 0, :]
    w_kv = w_kv_b.reshape(KV_LORA, N_HEADS_A, QK_NOPE + V_HEAD)
    w_uk = w_kv[..., :QK_NOPE]
    w_uv = w_kv[..., QK_NOPE:]
    q_lat = jnp.einsum('bthn,rhn->bthr', q_nope, w_uk)
    if ckv_past is None:
        o_lat = prompt_attention(q_lat, q_rope, ckv_new, kr_new)
    else:
        o_lat = mla_attend(q_lat, q_rope,
                           jnp.concatenate([ckv_past, ckv_new], axis=1),
                           jnp.concatenate([krope_past, kr_new], axis=1), None)
    o_a = jnp.einsum('bthr,rhv->bthv', o_lat, w_uv).reshape(b, t, WIDTH_A)
    y_a = rmsnorm(o_a * jax.nn.silu(g_a), ln_out_a)

    u = u_val * jax.nn.sigmoid(u_gate)
    if conv_past is None:
        past = jnp.zeros((b, CONV_STATE, CONV_CH), u.dtype)
    else:
        past = conv_past
    u_pad = jnp.concatenate([past, u], axis=1)
    v = causal_dwconv(u_pad, conv_w, conv_b)
    v = jax.nn.silu(layernorm(v, ln_conv_g, ln_conv_b))
    y_c = rmsnorm(v * jax.nn.silu(g_c), ln_out_c)
    conv_state = u_pad[:, -CONV_STATE:, :]

    h = h + jnp.concatenate([y_a, y_c], axis=-1) @ w_out
    gate = jax.nn.sigmoid(rmsnorm(h, ln_pg) @ w_pg)
    h = h + gate * (p @ w_pe)
    return h, ckv_new, kr_new, conv_state

def setup_inputs(seed: int = 0) -> dict:
    key = jax.random.key(seed)
    ks = jax.random.split(key, 24)
    f32 = jnp.float32

    def nrm(k, shape, scale=1.0):
        return jax.random.normal(k, shape, f32) * scale

    def gain(k, shape):
        return 1.0 + 0.05 * jax.random.normal(k, shape, f32)

    return {
        'x_prompt': nrm(ks[0], (BATCH, SEQ, D_MODEL)),
        'x_sample': nrm(ks[1], (DEC_BATCH, DEC_SEQ, D_MODEL)),
        'cache_ckv': nrm(ks[2], (DEPTH, DEC_BATCH, PAST_LEN, KV_LORA)),
        'cache_krope': nrm(ks[3], (DEPTH, DEC_BATCH, PAST_LEN, QK_ROPE)),
        'state_conv': nrm(ks[4], (DEPTH, DEC_BATCH, CONV_STATE, CONV_CH), 0.5),
        'p_prompt': nrm(ks[5], (DEPTH, BATCH, SEQ, D_PLE)),
        'p_sample': nrm(ks[6], (DEPTH, DEC_BATCH, DEC_SEQ, D_PLE)),
        'ln_in': gain(ks[7], (DEPTH, D_MODEL)),
        'w_in': nrm(ks[8], (DEPTH, D_MODEL, D_IN), D_MODEL ** -0.5),
        'ln_q': gain(ks[9], (DEPTH, Q_LORA)),
        'w_q_b': nrm(ks[10], (DEPTH, Q_LORA, N_HEADS_A * (QK_NOPE + QK_ROPE)), Q_LORA ** -0.5),
        'ln_kv': gain(ks[11], (DEPTH, KV_LORA)),
        'w_kv_b': nrm(ks[12], (DEPTH, KV_LORA, N_HEADS_A * (QK_NOPE + V_HEAD)), KV_LORA ** -0.5),
        'conv_w': nrm(ks[13], (DEPTH, CONV_W, CONV_CH), CONV_W ** -0.5),
        'conv_b': nrm(ks[14], (DEPTH, CONV_CH), 0.01),
        'ln_conv_g': gain(ks[15], (DEPTH, CONV_CH)),
        'ln_conv_b': nrm(ks[16], (DEPTH, CONV_CH), 0.01),
        'ln_out_a': gain(ks[17], (DEPTH, WIDTH_A)),
        'ln_out_c': gain(ks[18], (DEPTH, CONV_CH)),
        'w_out': nrm(ks[19], (DEPTH, D_MIX, D_MODEL), D_MIX ** -0.5),
        'w_pe': nrm(ks[20], (DEPTH, D_PLE, D_MODEL), D_PLE ** -0.5),
        'ln_pg': gain(ks[21], (DEPTH, D_MODEL)),
        'w_pg': nrm(ks[22], (DEPTH, D_MODEL, D_MODEL), D_MODEL ** -0.5),
        'ln_f': gain(ks[23], (D_MODEL,)),
    }

def reference(x_prompt, x_sample, cache_ckv, cache_krope, state_conv, p_prompt, p_sample,
              ln_in, w_in, ln_q, w_q_b, ln_kv, w_kv_b, conv_w, conv_b, ln_conv_g, ln_conv_b,
              ln_out_a, ln_out_c, w_out, w_pe, ln_pg, w_pg, ln_f):
    past_len = cache_ckv.shape[2]
    pos_p = jnp.arange(x_prompt.shape[1])
    pos_s = past_len + jnp.arange(x_sample.shape[1])
    h_p = x_prompt
    h_s = x_sample
    ckv_p, kr_p, cv_p, ckv_s, kr_s, cv_s = [], [], [], [], [], []
    for i in range(DEPTH):
        lw = (ln_in[i], w_in[i], ln_q[i], w_q_b[i], ln_kv[i], w_kv_b[i], conv_w[i], conv_b[i],
              ln_conv_g[i], ln_conv_b[i], ln_out_a[i], ln_out_c[i], w_out[i], w_pe[i],
              ln_pg[i], w_pg[i])
        h_p, a, b_, c = mixer_layer(h_p, p_prompt[i], pos_p, None, None, None, *lw)
        ckv_p.append(a)
        kr_p.append(b_)
        cv_p.append(c)
        h_s, a, b_, c = mixer_layer(h_s, p_sample[i], pos_s, cache_ckv[i], cache_krope[i],
                                    state_conv[i], *lw)
        ckv_s.append(a)
        kr_s.append(b_)
        cv_s.append(c)
    y_prompt = rmsnorm(h_p, ln_f)
    y_sample = rmsnorm(h_s, ln_f)
    return (y_prompt, y_sample,
            jnp.stack(ckv_p), jnp.stack(kr_p), jnp.stack(cv_p),
            jnp.stack(ckv_s), jnp.stack(kr_s), jnp.stack(cv_s))


_drawn_inputs = setup_inputs


def setup_inputs(seed=0):
    import zlib

    import numpy as np

    out = dict(_drawn_inputs(seed))
    spreads = {}
    factors = {'conv_b': 3.813, 'ln_conv_b': 7.398, 'ln_pg': 5.656}
    for name, (base, spread) in spreads.items():
        noise = np.random.default_rng([zlib.crc32(name.encode()), seed]).standard_normal(out[name].shape)
        drawn = base * np.exp(spread * noise) if base else spread * noise
        out[name] = __import__('jax').numpy.asarray(drawn.astype(out[name].dtype))
    for name, factor in factors.items():
        out[name] = (out[name] * factor).astype(out[name].dtype)
    return out
```

```python
from contextlib import ExitStack

import concourse.bass as bass
from concourse import mybir

ALU = mybir.AluOpType
ACT = mybir.ActivationFunctionType
F32 = mybir.dt.float32
I32 = mybir.dt.int32
BF16 = mybir.dt.bfloat16

P = 128
D = 1024
SEQ = 512
DEPTH = 2
NB, NS, PAST = 8, 16, 256
PLE = 256
HEADS, NOPE, ROPE, VH = 8, 64, 32, 64
LORA, QLORA = 128, 256
CH, TAPS = 512, 31
STATE = TAPS - 1
SCALE = float(NOPE + ROPE) ** -0.5
EPS = 1e-6
NEG = -1e30
TILES = SEQ // P + 1
TOK = TILES * P
KT = D // P
RING = 3
NZ = QLORA + LORA + ROPE
MAGIC = float(0x5F3759DF)

BLOCKS = ["zA", "uv", "ug", "ga", "gc", "pe0", "pe1", "o0", "o1", "pg0", "pg1"]
BLK = {name: i for i, name in enumerate(BLOCKS)}
ZCOL = {"zA": (0, NZ), "ga": (NZ, 512), "uv": (NZ + 512, 512), "ug": (NZ + 1024, 512), "gc": (NZ + 1536, 512)}


def weight_chunks():
    out = [(b, c) for b in ("zA", "uv", "ug", "ga", "gc") for c in range(2)]
    out += [("pe", 0)]
    return out + [(b, c) for b in ("o0", "o1", "pg0", "pg1") for c in range(2)]


CHUNKS = weight_chunks()
CHUNK = {c: i for i, c in enumerate(CHUNKS)}
UNITS = HEADS * (SEQ // P)
FILL_S = {s: s for s in range(NB)}
FILL_P = {(k * 8) // 3: NB + k for k in range(20 - NB)}
TAP_S = {s: [s] for s in range(NB)}
TAP_P = {}
_left = list(range(NB, TAPS))
for _u in range(UNITS):
    if _u % 4 != 3 and _left:
        TAP_P[_u] = [_left.pop(0)]


def shared_bank_plan():
    order = {"S": [], "T": [], "O": []}
    turn = [0]

    def cyc(*names):
        for n in names:
            order["STO"[turn[0] % 3]].append(n)
            turn[0] += 1

    cyc("gain", "taps")
    for t in range(TILES):
        for g in range(2):
            cyc(("x", t, g))
    cyc("uk0", "uk1", "st0", "st1", "p0", "p1", "p2")
    for t in range(TILES):
        cyc(("small", t))
    cyc("qs0", "qs1", "ql0", "ql1")
    for t in range(TILES):
        cyc(("u", t))
    order["T"].append(("c", 0))
    for s in range(NB):
        order["S"].append(("s", s))
        order["O"].append(("o", s))
        if s < NB - 1:
            order["T"].append(("c", s + 1))
        order["T"].append(("p", s))
    for j in range(4):
        cyc(("v", j))
    order["S"].append("oa")
    order["T"] += [("k", 0), ("q", 0)]
    for u in range(UNITS):
        h, i = divmod(u, 4)
        order["S"].append(("s", NB + u))
        if i == 0:
            order["O"].append(("oh", h))
        if i == 1 and h < HEADS - 1:
            order["T"].append(("k", h + 1))
        if i == 2 and h < HEADS - 1:
            order["T"].append(("q", h + 1))
        order["T"].append(("p", NB + u))
    for t in range(TILES):
        cyc(("cv", t))
    for n in ("y", "h"):
        for t in range(TILES):
            for g in range(2):
                cyc((n, t, g))
    return {n: (b, i) for b, names in order.items() for i, n in enumerate(names)}


def build(nc, a):
    ctx = ExitStack()
    plan = shared_bank_plan()
    with ctx:
        def sb(name, shape, dt=F32):
            return ctx.enter_context(nc.sbuf_tensor(name, shape, dt))

        H = sb("H", [P, TILES, D])
        XT = sb("XT", [P, TILES, KT, P])
        WR = sb("WR", [P, RING, 2048])
        Y = sb("Y", [P, TILES, D])
        OTOK = sb("OTOK", [P, TILES, 512])
        PTR = sb("PTR", [P, 2, TOK])
        UT = sb("UT", [P, 4, STATE + SEQ])
        UTS = sb("UTS", [P, 4, NB, STATE + NS])
        VT = sb("VT", [P, 4 * TOK])
        VTv = VT[:, :].rearrange("p (c t) -> p c t", c=4)
        WQ = sb("WQ", [P, 2, HEADS, 128])
        WKV = sb("WKV", [P, HEADS, 128])
        Z = sb("Z", [P, TILES, NZ + ROPE])
        CQT = sb("CQT", [P, 2, TOK])
        CKVT = sb("CKVT", [P, TOK])
        KRS = sb("KRS", [P, P])
        V = sb("V", [P, 4, 512])
        QL = V[:, 0:2, :].rearrange("p a (s h t) -> p (a s) h t", h=HEADS, t=NS)
        OL = sb("OL", [P, HEADS, P])
        UKT = OL
        KH = sb("KH", [P, 2, 512])
        QH = sb("QH", [P, 2, 512])
        QS = QH[:, :, :].rearrange("p a (s h t) -> p (a s) h t", h=HEADS, t=NS)
        SB = sb("SB", [P, 2, 512])
        PT = sb("PT", [P, 2, 4, P])
        CKV = sb("CKV", [P, 2, 2, LORA])
        CKR = sb("CKR", [P, 2, 2, 128])
        CTK = sb("CTK", [P, 512])
        TH = sb("TH", [P, 2, 512])
        ROWS = sb("ROWS", [30, P])
        GT = sb("GT", [P, 30])
        CWT = sb("CWT", [P, 4, TAPS])
        LNKV = sb("LNKV", [P, LORA])
        LCG = sb("LCG", [P, CH])
        LCB = sb("LCB", [P, CH])
        IDENT = sb("IDENT", [P, P])
        ROPET = sb("ROPET", [P, TOK])
        ROPEK = sb("ROPEK", [P, TILES, 4, 16])
        MASK = sb("MASK", [P, 512])
        MROW = sb("MROW", [1, 240])
        ONES = sb("ONES", [1, P])
        JUNK = sb("JUNK", [P, D], BF16)
        MS = sb("MS", [P, 32])
        RS = sb("RS", [P, 32])
        HR = sb("HR", [P, 8])
        NR = sb("NR", [P, 3, 16])
        RSV = sb("RSV", [P, TILES])
        KRA = sb("KRA", [P, TILES, 2, 16])
        KRB = sb("KRB", [P, TILES, 2, 16])
        NBIAS = sb("NBIAS", [P, NB + UNITS])
        SUMS = sb("SUMS", [P, NB + UNITS])
        RSUM = sb("RSUM", [P, NB + UNITS])
        BN6 = sb("BN6", [P, TILES, 6])
        MV = sb("MV", [P, TILES, 2])

        G_IN, G_PG, G_OUT, G_Q, G_CB = 0, 8, 16, 24, 26

        acc = [ctx.enter_context(nc.psum_tensor(f"acc{t}", [P, 512], F32)) for t in range(TILES)]
        shared = {b: ctx.enter_context(nc.psum_tensor(f"shared{b}", [P, 512], F32)) for b in "STO"}

        sems = []

        def sem(name):
            s = ctx.enter_context(nc.semaphore(name))
            sems.append(s)
            return s

        filled = {b: sem(f"filled_{b}") for b in "STO"}
        drained = {b: sem(f"drained_{b}") for b in "STO"}
        acc_filled = [sem(f"acc_filled{t}") for t in range(TILES)]
        acc_drained = [sem(f"acc_drained{t}") for t in range(TILES)]
        w_loaded = [sem(f"w_loaded{i}") for i in range(RING)]
        first_half_used = sem("first_half_used")
        rows_in = sem("rows_in")
        taps_in = sem("taps_in")
        state_in = sem("state_in")
        p_in = sem("p_in")
        wq_in = sem("wq_in")
        wq_rot = sem("wq_rot")
        wkv_in = sem("wkv_in")
        lnkv_in = sem("lnkv_in")
        lnconv_in = sem("lnconv_in")
        cache_in = [sem(f"cache_in{i}") for i in range(2)]
        squares = sem("squares")
        rstd_ready = sem("rstd_ready")
        cq_scaled = sem("cq_scaled")
        latents_ready = sem("latents_ready")
        gated = sem("gated")
        exped = sem("exped")
        p_scaled = sem("p_scaled")
        conv_done = sem("conv_done")
        ln_scaled = sem("ln_scaled")
        ln_done = sem("ln_done")
        v_tanh = sem("v_tanh")
        ya_ready = sem("ya_ready")
        yc_ready = sem("yc_ready")
        ya_scaled = sem("ya_scaled")
        yc_scaled = sem("yc_scaled")
        h_done = sem("h_done")
        latents_stored = sem("latents_stored")
        u_stored = sem("u_stored")
        states_stored = sem("states_stored")
        dve_chain = sem("dve_chain")
        act_chain = sem("act_chain")
        const_in = sem("const_in")
        const_set = sem("const_set")
        y_stored = sem("y_stored")

        def bank(name):
            return shared[plan[name][0]]

        def fill_wait(eng, name):
            b, i = plan[name]
            if i:
                eng.wait_ge(drained[b], i)

        def fill_inc(ins, name):
            ins.then_inc(filled[plan[name][0]], 1)

        def filled_wait(eng, name):
            b, i = plan[name]
            eng.wait_ge(filled[b], i + 1)

        def drain_inc(ins, name):
            ins.then_inc(drained[plan[name][0]], 1)

        def copied_wait(eng, name):
            b, i = plan[name]
            eng.wait_ge(drained[b], i + 1)

        class Chain:

            def __init__(self, eng, s):
                self.eng, self.s, self.n = eng, s, 0

            def link(self, ins):
                self.n += 1
                ins.then_inc(self.s, 1)
                self.eng.wait_ge(self.s, self.n)

        def rsqrt(eng, chain, src, dst, n):
            half = NR[:, 0, 0:n]
            tmp = NR[:, 1, 0:n]
            x = NR[:, 2, 0:n]
            chain.link(eng.tensor_scalar(x, src, EPS, None, ALU.add))
            chain.link(eng.tensor_scalar(half, x, -0.5, None, ALU.mult))
            chain.link(eng.tensor_scalar(dst.bitcast(I32), x.bitcast(I32), -0.5, MAGIC, ALU.mult, ALU.add))
            for k in range(3):
                chain.link(eng.tensor_tensor(tmp, dst, dst, ALU.mult))
                chain.link(eng.tensor_tensor(tmp, tmp, half, ALU.mult))
                last = eng.scalar_tensor_tensor(out=dst, in0=tmp, scalar=1.5, in1=dst, op0=ALU.add, op1=ALU.mult)
                if k < 2:
                    chain.link(last)
            return last

        with nc.Block() as block:
            @block.sync
            def _(sp):
                sp.dma_start(H[:, 0:4, :], a["x_prompt"].rearrange("o (t p) d -> p (o t) d", p=P)).then_inc(const_in, 16)
                sp.dma_start(H[:, 4, :], a["x_sample"].rearrange("b s d -> (b s) d")).then_inc(const_in, 16)
                sp.dma_start(IDENT[:, :], a["c_ident"]).then_inc(const_in, 16)
                sp.dma_start(ROPET[:, :], a["c_ropet"]).then_inc(const_in, 16)
                sp.dma_start(ROPEK[:, :, :, :], a["c_ropek"]).then_inc(const_in, 16)
                sp.dma_start(MASK[:, :], a["c_mask"]).then_inc(const_in, 16)
                sp.dma_start(MROW[:, :], a["c_mrow"]).then_inc(const_in, 16)
                sp.wait_ge(const_in, 16 * 7)

            @block.gpsimd
            def _(pool):
                nc.gpsimd.memset(UT[:, :, 0:STATE], 0.0).then_inc(const_set, 1)
                nc.gpsimd.memset(CKR[:, :, :, 0:NOPE], 0.0).then_inc(const_set, 1)
                nc.gpsimd.memset(ONES[:, :], 1.0).then_inc(const_set, 1)

        with nc.Fori(0, DEPTH) as layer:
            def at(name):
                return a[name][bass.ds(layer, 1)]

            with nc.Block() as block:
                @block.sync
                def _(sp):
                    for name, g, n in (("ln_in", G_IN, 8), ("ln_pg", G_PG, 8), ("ln_out_a", G_OUT, 4),
                                       ("ln_out_c", G_OUT + 4, 4), ("ln_q", G_Q, 2), ("conv_b", G_CB, 4)):
                        sp.dma_start(ROWS[g:g + n, :], at(name).rearrange("o (k p) -> (o k) p", p=P)).then_inc(rows_in, 16)

                    def chunk(j):
                        name, c = CHUNKS[j]
                        if j >= RING:
                            before, half = CHUNKS[j - RING]
                            if before == "pe":
                                sp.wait_ge(acc_filled[TILES - 1], BLK["pe1"] + 1)
                            elif half:
                                sp.wait_ge(acc_filled[TILES - 1], BLK[before] + 1)
                            else:
                                sp.wait_ge(first_half_used, sum(x != "pe" and y == 0 for x, y in CHUNKS[:j - RING + 1]))
                        slot = WR[:, j % RING, :]
                        if name in ZCOL:
                            col, n = ZCOL[name]
                            src = at("w_in")[:, 512 * c:512 * (c + 1), col:col + n]
                            dst = slot[:, 0:4 * n].rearrange("p (k n) -> p k n", k=4)
                        elif name == "pe":
                            src = at("w_pe")
                            dst = slot.rearrange("p (k n) -> p k n", k=2)
                        else:
                            w = "w_out" if name[0] == "o" else "w_pg"
                            half = int(name[-1])
                            src = at(w)[:, 512 * c:512 * (c + 1), 512 * half:512 * (half + 1)]
                            dst = slot.rearrange("p (k n) -> p k n", k=4)
                        sp.dma_start(dst, src.rearrange("o (k p) n -> p (o k) n", p=P)).then_inc(w_loaded[j % RING], 16)

                    sp.dma_start(VT[0:TAPS, 1024:1536], at("conv_w").rearrange("o k c -> (o k) c")).then_inc(taps_in, 16)
                    chunk(0)
                    chunk(1)
                    sp.dma_start(WKV[:, :, :], at("w_kv_b").rearrange("o r (h e) -> (o r) h e", e=128)).then_inc(wkv_in, 16)
                    sp.dma_start(VT[0:120, 0:1024].rearrange("p (a c) -> p a c", a=2),
                                 at("state_conv").rearrange("o (a b) j c -> (b j) (o a) c", a=2)).then_inc(state_in, 16)
                    sp.dma_start(OTOK[:, 0:4, 0:PLE], at("p_prompt").rearrange("l o (t p) d -> p (l o t) d", p=P)).then_inc(p_in, 16)
                    sp.dma_start(OTOK[:, 4, 0:PLE], at("p_sample").rearrange("o b s d -> (o b s) d")).then_inc(p_in, 16)
                    chunk(2)
                    for k in range(2):
                        sp.dma_start(WQ[:, k, :, 0:NOPE + ROPE],
                                     at("w_q_b")[:, P * k:P * (k + 1), :].rearrange("o p (h e) -> (o p) h e", h=HEADS)).then_inc(wq_in, 16)
                    sp.dma_start(LNKV[:, :], at("ln_kv").to_broadcast([P, LORA])).then_inc(lnkv_in, 16)
                    sp.dma_start(LCG[:, :], at("ln_conv_g").to_broadcast([P, CH])).then_inc(lnconv_in, 16)
                    sp.dma_start(LCB[:, :], at("ln_conv_b").to_broadcast([P, CH])).then_inc(lnconv_in, 16)
                    for j in range(3, len(CHUNKS)):
                        chunk(j)

                @block.tensor
                def _(pe):
                    mm = nc.tensor.matmul

                    def flip(out, in_):
                        rows = in_.shape[0]
                        return nc.tensor.transpose(out, in_, IDENT[0:rows, 0:rows])

                    def quad(name):
                        return bank(name)[:, :].rearrange("p (j t) -> p j t", t=P)

                    fill_wait(pe, "gain")
                    pe.wait_ge(rows_in, 16 * 6)
                    fill_inc(flip(bank("gain")[:, 0:30], ROWS[:, :]), "gain")
                    fill_wait(pe, "taps")
                    pe.wait_ge(taps_in, 16)
                    for c in range(4):
                        last = flip(bank("taps")[:, TAPS * c:TAPS * (c + 1)], VT[0:TAPS, 1024 + P * c:1024 + P * (c + 1)])
                    fill_inc(last, "taps")

                    def flip_half(name, src):
                        g = name[2]
                        fill_wait(pe, name)
                        for j in range(4):
                            last = flip(quad(name)[:, j, :], src[:, P * (4 * g + j):P * (4 * g + j + 1)])
                        fill_inc(last, name)

                    for t in range(TILES):
                        for g in range(2):
                            flip_half(("x", t, g), H[:, t, :])
                    pe.wait_ge(wkv_in, 16)
                    for g in range(2):
                        name = f"uk{g}"
                        fill_wait(pe, name)
                        for j in range(4):
                            last = flip(quad(name)[0:NOPE, j, :], WKV[:, 4 * g + j, 0:NOPE])
                        fill_inc(last, name)
                    pe.wait_ge(state_in, 16)
                    for g in range(2):
                        name = f"st{g}"
                        fill_wait(pe, name)
                        for c in range(4):
                            last = flip(bank(name)[:, 120 * c:120 * (c + 1)], VT[0:120, 512 * g + P * c:512 * g + P * (c + 1)])
                        fill_inc(last, name)
                    pe.wait_ge(p_in, 32)
                    for g in range(3):
                        name = f"p{g}"
                        fill_wait(pe, name)
                        for j, t in enumerate(range(2 * g, min(2 * g + 2, TILES))):
                            for k in range(2):
                                last = flip(quad(name)[:, 2 * j + k, :], OTOK[:, t, P * k:P * (k + 1)])
                        fill_inc(last, name)

                    def quantum(name, c, t):
                        j = CHUNK[(name, c)]
                        n = NZ if name == "zA" else 512
                        w = WR[:, j % RING, 0:4 * n].rearrange("p (k n) -> p k n", k=4)
                        if t == 0:
                            pe.wait_ge(w_loaded[j % RING], 16 * (j // RING + 1))
                        if c == 0:
                            if BLK[name]:
                                pe.wait_ge(acc_drained[t], BLK[name])
                        for k in range(4):
                            last = mm(acc[t][:, 0:n], XT[:, t, 4 * c + k, :], w[:, k, :],
                                      start=(c == 0 and k == 0), stop=(c == 1 and k == 3))
                        if c == 1:
                            last.then_inc(acc_filled[t], 1)
                        elif t == TILES - 1:
                            last.then_inc(first_half_used, 1)

                    for name in ("zA", "uv"):
                        for c in range(2):
                            for t in range(TILES):
                                if name == "zA" and c == 0:
                                    copied_wait(pe, ("x", t, 0))
                                    copied_wait(pe, ("x", t, 1))
                                quantum(name, c, t)

                    pe.wait_ge(latents_ready, 1)
                    for t in range(TILES):
                        name = ("small", t)
                        fill_wait(pe, name)
                        pe.wait_ge(cq_scaled, t + 1)
                        for k in range(2):
                            flip(quad(name)[:, k, :], Z[:, t, P * k:P * (k + 1)])
                        flip(quad(name)[:, 2, :], Z[:, t, QLORA:QLORA + LORA])
                        fill_inc(flip(quad(name)[:, 3, :], Z[:, t, NZ + ROPE - P:NZ + ROPE]), name)

                    for c in range(2):
                        for t in range(TILES):
                            quantum("ug", c, t)

                    pe.wait_ge(wq_rot, 2)
                    pe.wait_ge(wq_in, 32)
                    for t in range(TILES):
                        copied_wait(pe, ("small", t))
                    for g in range(2):
                        name = f"qs{g}"
                        fill_wait(pe, name)
                        for j in range(4):
                            for k in range(2):
                                last = mm(quad(name)[:, j, :], WQ[:, k, 4 * g + j, :], CQT[:, k, SEQ:TOK],
                                          start=(k == 0), stop=(k == 1))
                        fill_inc(last, name)
                    copied_wait(pe, "uk0")
                    copied_wait(pe, "uk1")
                    for g in range(2):
                        name = f"ql{g}"
                        fill_wait(pe, name)
                        copied_wait(pe, f"qs{g}")
                        for j in range(4):
                            last = mm(quad(name)[:, j, :], UKT[0:NOPE, 4 * g + j, :], QS[0:NOPE, :, 4 * g + j, :],
                                      start=True, stop=True)
                        fill_inc(last, name)
                    for t in range(TILES):
                        name = ("u", t)
                        fill_wait(pe, name)
                        pe.wait_ge(gated, t + 1)
                        for c in range(4):
                            last = flip(quad(name)[:, c, :], Y[:, t, 512 + P * c:512 + P * (c + 1)])
                        fill_inc(last, name)

                    def filler(q):
                        name, q = ("ga", q) if q < 10 else ("gc", q - 10)
                        quantum(name, q // 5, q % 5)

                    def flip_cache(s):
                        name = ("c", s)
                        fill_wait(pe, name)
                        pe.wait_ge(cache_in[s % 2], 48 * (s // 2 + 1))
                        for j in range(2):
                            flip(quad(name)[:, j, :], CKV[:, s % 2, j, :])
                            last = flip(quad(name)[:, 2 + j, :], CKR[:, s % 2, j, :])
                        fill_inc(last, name)

                    def flip_probs(n, w):
                        name = ("p", n)
                        fill_wait(pe, name)
                        for j in range(w // P):
                            last = flip(quad(name)[:, j, :], SB[:, n % 2, P * j:P * (j + 1)])
                        fill_inc(last, name)

                    def sample_values(s):
                        name = ("o", s)
                        fill_wait(pe, name)
                        copied_wait(pe, ("p", s))
                        out = bank(name)[:, 0:P]
                        for j in range(2):
                            mm(out, CKV[:, s % 2, j, :], PT[:, s % 2, j, :], start=(j == 0), stop=False)
                        fill_inc(mm(out, Z[:, TILES - 1, QLORA:QLORA + LORA], PT[:, s % 2, 2, :],
                                    start=False, stop=True), name)

                    copied_wait(pe, "ql1")
                    flip_cache(0)
                    for s in range(NB):
                        name = ("s", s)
                        fill_wait(pe, name)
                        copied_wait(pe, ("c", s))
                        q_lat = QL[:, s, :, :].rearrange("p h t -> p (h t)")
                        q_rot = QS[NOPE:P, s, :, :].rearrange("p h t -> p (h t)")
                        mm(bank(name)[:, 0:PAST], q_lat, CTK[:, 0:PAST], start=True, stop=False)
                        mm(bank(name)[:, 0:PAST], q_rot, CTK[NOPE:P, PAST:2 * PAST], start=False, stop=True)
                        new = bank(name)[:, PAST:PAST + P]
                        mm(new, q_lat, CKVT[:, SEQ:TOK], start=True, stop=False)
                        mm(new, q_rot, KRS[NOPE:P, :], start=False, stop=False)
                        fill_inc(mm(new, ONES[:, :], MROW[:, 112 - NS * s:240 - NS * s], start=False, stop=True), name)
                        if s:
                            sample_values(s - 1)
                        if s < NB - 1:
                            flip_cache(s + 1)
                        filler(FILL_S[s])
                        pe.wait_ge(p_scaled, s + 1)
                        flip_probs(s, PAST + P)
                    sample_values(NB - 1)

                    for j in range(4):
                        name = ("v", j)
                        fill_wait(pe, name)
                        fill_inc(mm(bank(name)[:, :], CKVT[:, P * j:P * (j + 1)], WKV[:, :, NOPE:P], start=True, stop=True), name)
                    fill_wait(pe, "oa")
                    copied_wait(pe, ("o", NB - 1))
                    for h in range(HEADS):
                        last = mm(bank("oa")[:, VH * h:VH * (h + 1)], OL[:, h, :], WKV[:, h, NOPE:P], start=True, stop=True)
                    fill_inc(last, "oa")

                    def keys(h):
                        name = ("k", h)
                        fill_wait(pe, name)
                        fill_inc(mm(bank(name)[0:NOPE, :], WKV[:, h, 0:NOPE], CKVT[:, 0:SEQ], start=True, stop=True), name)

                    def queries(h):
                        name = ("q", h)
                        fill_wait(pe, name)
                        for k in range(2):
                            last = mm(bank(name)[:, :], WQ[:, k, h, :], CQT[:, k, 0:SEQ], start=(k == 0), stop=(k == 1))
                        fill_inc(last, name)

                    def scores(u):
                        h, i = divmod(u, 4)
                        name = ("s", NB + u)
                        fill_wait(pe, name)
                        if i == 0:
                            copied_wait(pe, ("k", h))
                            copied_wait(pe, ("q", h))
                        w = P * (i + 1)
                        fill_inc(mm(bank(name)[:, 0:w], QH[:, h % 2, P * i:P * (i + 1)], KH[:, h % 2, 0:w],
                                    start=True, stop=True), name)

                    def values(u):
                        h, i = divmod(u, 4)
                        n = NB + u
                        name = ("oh", h)
                        if i == 0:
                            fill_wait(pe, name)
                        copied_wait(pe, ("p", n))
                        for j in range(i + 1):
                            last = mm(quad(name)[:, i, :], PT[:, n % 2, j, :], V[:, j, P * (h // 2):P * (h // 2 + 1)],
                                      start=(j == 0), stop=(j == i))
                        if i == 3:
                            fill_inc(last, name)

                    keys(0)
                    queries(0)
                    for j in range(4):
                        copied_wait(pe, ("v", j))
                    scores(0)
                    for u in range(UNITS):
                        h, i = divmod(u, 4)
                        if u < UNITS - 1:
                            scores(u + 1)
                        if u:
                            values(u - 1)
                        if i == 1 and h < HEADS - 1:
                            keys(h + 1)
                        if i == 2 and h < HEADS - 1:
                            queries(h + 1)
                        if u in FILL_P:
                            filler(FILL_P[u])
                        pe.wait_ge(exped, NB + u + 1)
                        flip_probs(NB + u, P * (i + 1))
                    values(UNITS - 1)

                    pe.wait_ge(conv_done, 8 * TAPS)
                    for t in range(TILES):
                        name = ("cv", t)
                        fill_wait(pe, name)
                        for c in range(4):
                            last = flip(quad(name)[:, c, :], VTv[:, c, P * t:P * (t + 1)])
                        fill_inc(last, name)
                    for g in range(3):
                        copied_wait(pe, f"p{g}")
                    j = CHUNK[("pe", 0)]
                    pe.wait_ge(w_loaded[j % RING], 16 * (j // RING + 1))
                    w = WR[:, j % RING, :].rearrange("p (k n) -> p k n", k=2)
                    for half in range(2):
                        for t in range(TILES):
                            pe.wait_ge(acc_drained[t], BLK["pe0"] + half)
                            for k in range(2):
                                last = mm(acc[t][:, :], PTR[:, k, P * t:P * (t + 1)], w[:, k, 512 * half:512 * (half + 1)],
                                          start=(k == 0), stop=(k == 1))
                            last.then_inc(acc_filled[t], 1)

                    for t in range(TILES):
                        pe.wait_ge(ya_scaled, t + 1)
                        flip_half(("y", t, 0), Y[:, t, :])
                        pe.wait_ge(yc_scaled, t + 1)
                        flip_half(("y", t, 1), Y[:, t, :])
                    for name in ("o0", "o1"):
                        for c in range(2):
                            for t in range(TILES):
                                if name == "o0":
                                    copied_wait(pe, ("y", t, c))
                                quantum(name, c, t)
                                if name == "o1" and c == 1 and t >= 2:
                                    flip_new_h = t - 2
                                    pe.wait_ge(acc_drained[flip_new_h], BLK["o1"] + 1)
                                    flip_half(("h", flip_new_h, 0), H[:, flip_new_h, :])
                                    flip_half(("h", flip_new_h, 1), H[:, flip_new_h, :])
                    for t in range(TILES - 2, TILES):
                        pe.wait_ge(acc_drained[t], BLK["o1"] + 1)
                        flip_half(("h", t, 0), H[:, t, :])
                        flip_half(("h", t, 1), H[:, t, :])
                    for name in ("pg0", "pg1"):
                        for c in range(2):
                            for t in range(TILES):
                                if name == "pg0":
                                    copied_wait(pe, ("h", t, c))
                                quantum(name, c, t)

                @block.scalar
                def _(act):
                    av = nc.scalar.activation
                    th = [0]
                    n_sq = [0]

                    def mean_square(src, col, n, scale=1.0):
                        if n_sq[0]:
                            act.wait_ge(squares, n_sq[0])
                        n_sq[0] += 1
                        av(JUNK[:, 0:n], src, ACT.Square, scale=scale * n ** -0.5,
                           accum_out=MS[:, col:col + 1]).then_inc(squares, 1)

                    def copy(out, in_, scale=None):
                        return av(out, in_, ACT.Copy) if scale is None else av(out, in_, ACT.Copy, scale=scale)

                    def quad(name):
                        return bank(name)[:, :].rearrange("p (j t) -> p j t", t=P)

                    for t in range(TILES):
                        mean_square(H[:, t, :], t, D)
                    for g in range(2):
                        name = f"uk{g}"
                        filled_wait(act, name)
                        drain_inc(copy(UKT[0:NOPE, 4 * g:4 * g + 4, :], quad(name)[0:NOPE, :, :]), name)
                    for g in range(2):
                        name = f"st{g}"
                        filled_wait(act, name)
                        for c in range(4):
                            last = copy(UTS[:, c, 4 * g:4 * g + 4, 0:STATE],
                                        bank(name)[:, 120 * c:120 * (c + 1)].rearrange("p (b j) -> p b j", b=4))
                        drain_inc(last, name)
                    for g in range(3):
                        name = f"p{g}"
                        filled_wait(act, name)
                        m = min(2, TILES - 2 * g)
                        for k in range(2):
                            src = bank(name)[:, 0:2 * P * m].rearrange("p (t k e) -> p k t e", k=2, e=P)[:, k]
                            last = copy(PTR[:, k, 2 * P * g:2 * P * g + P * m].rearrange("p (t e) -> p t e", e=P), src)
                        drain_inc(last, name)

                    act.wait_ge(wq_in, 32)
                    copy(WQ[:, :, :, 96:112], WQ[:, :, :, 80:96]).then_inc(wq_rot, 1)
                    copy(WQ[:, :, :, 112:128], WQ[:, :, :, 64:80]).then_inc(wq_rot, 1)

                    act.wait_ge(rstd_ready, 1)
                    for t in range(TILES):
                        act.wait_ge(acc_filled[t], BLK["zA"] + 1)
                        copy(Z[:, t, 0:NZ], acc[t][:, 0:NZ], RS[:, t:t + 1]).then_inc(acc_drained[t], 1)
                    for t in range(TILES):
                        act.wait_ge(acc_drained[t], BLK["zA"] + 1)
                        mean_square(Z[:, t, 0:QLORA], 5 + t, QLORA)
                        mean_square(Z[:, t, QLORA:QLORA + LORA], 10 + t, LORA)
                    act.wait_ge(rstd_ready, 2)
                    for t in range(TILES):
                        copy(Z[:, t, 0:QLORA], Z[:, t, 0:QLORA], RS[:, 5 + t:6 + t]).then_inc(cq_scaled, 1)
                    for t in range(TILES):
                        act.wait_ge(acc_filled[t], BLK["uv"] + 1)
                        copy(Y[:, t, 512:1024], acc[t][:, :], HR[:, t:t + 1]).then_inc(acc_drained[t], 1)
                    for t in range(TILES):
                        name = ("small", t)
                        filled_wait(act, name)
                        cols = slice(P * t, P * (t + 1))
                        for k in range(2):
                            copy(CQT[:, k, cols], quad(name)[:, k, :], GT[:, G_Q + k:G_Q + k + 1])
                        copy(CKVT[:, cols], quad(name)[:, 2, :])
                        if t < TILES - 1:
                            copy(KH[NOPE:P, 0, cols], quad(name)[NOPE:P, 3, :])
                            drain_inc(copy(KH[NOPE:P, 1, cols], quad(name)[NOPE:P, 3, :]), name)
                        else:
                            drain_inc(copy(KRS[NOPE:P, :], quad(name)[NOPE:P, 3, :]), name)

                    def tanh_acc(t, block_no, hr):
                        k = th[0]
                        th[0] += 1
                        if k >= 2:
                            act.wait_ge(gated, k - 1)
                        av(TH[:, k % 2, :], acc[t][:, :], ACT.Tanh, scale=hr).then_inc(acc_drained[t], 1)

                    for t in range(TILES):
                        act.wait_ge(acc_filled[t], BLK["ug"] + 1)
                        tanh_acc(t, BLK["ug"], HR[:, t:t + 1])
                    for g in range(2):
                        name = f"ql{g}"
                        filled_wait(act, name)
                        for j in range(4):
                            last = copy(QL[:, :, 4 * g + j, :], quad(name)[:, j, :].rearrange("p (s t) -> p s t", t=NS))
                        drain_inc(last, name)
                    for t in range(TILES):
                        name = ("u", t)
                        filled_wait(act, name)
                        if t < TILES - 1:
                            drain_inc(copy(UT[:, :, STATE + P * t:STATE + P * (t + 1)], quad(name)), name)
                        else:
                            for c in range(4):
                                last = copy(UTS[:, c, :, STATE:STATE + NS],
                                            quad(name)[:, c, :].rearrange("p (b j) -> p b j", b=NB))
                            drain_inc(last, name)

                    def filler_out(q):
                        name, q = ("ga", q) if q < 10 else ("gc", q - 10)
                        if q < 5:
                            return
                        t = q - 5
                        act.wait_ge(acc_filled[t], BLK[name] + 1)
                        if name == "gc" and t == 0:
                            act.wait_ge(u_stored, 16 * (1 + NB))
                        col = 0 if name == "ga" else 512
                        copy(Y[:, t, col:col + 512], acc[t][:, :], HR[:, t:t + 1])
                        tanh_acc(t, BLK[name], HR[:, t:t + 1])

                    def probs(n, w):
                        copied_wait(act, ("s", n))
                        av(SB[:, n % 2, 0:w], SB[:, n % 2, 0:w], ACT.Exp, scale=-1.0, bias=NBIAS[:, n:n + 1],
                           accum_out=SUMS[:, n:n + 1]).then_inc(exped, 1)

                    def probs_out(n, k):
                        name = ("p", n)
                        filled_wait(act, name)
                        drain_inc(copy(PT[:, n % 2, 0:k, :], quad(name)[:, 0:k, :]), name)

                    def cache_out(s):
                        name = ("c", s)
                        filled_wait(act, name)
                        drain_inc(copy(CTK[:, :], bank(name)[:, :]), name)

                    def sample_out(s):
                        name = ("o", s)
                        filled_wait(act, name)
                        drain_inc(copy(OL[:, :, NS * s:NS * (s + 1)],
                                       bank(name)[:, 0:P].rearrange("p (h t) -> p h t", h=HEADS)), name)

                    cache_out(0)
                    for s in range(NB):
                        if s:
                            sample_out(s - 1)
                        if s < NB - 1:
                            cache_out(s + 1)
                        probs(s, PAST + P)
                        filler_out(FILL_S[s])
                        probs_out(s, 3)
                    sample_out(NB - 1)
                    for j in range(4):
                        name = ("v", j)
                        filled_wait(act, name)
                        drain_inc(copy(V[:, j, :], bank(name)[:, :]), name)
                    filled_wait(act, "oa")
                    drain_inc(copy(OTOK[:, TILES - 1, :], bank("oa")[:, :]), "oa")

                    def keys_out(h):
                        name = ("k", h)
                        filled_wait(act, name)
                        drain_inc(copy(KH[0:NOPE, h % 2, :], bank(name)[0:NOPE, :]), name)

                    keys_out(0)
                    for u in range(UNITS):
                        h, i = divmod(u, 4)
                        if i == 1 and h < HEADS - 1:
                            keys_out(h + 1)
                        probs(NB + u, P * (i + 1))
                        if u in FILL_P:
                            filler_out(FILL_P[u])
                        probs_out(NB + u, i + 1)

                    for t in range(TILES):
                        act.wait_ge(ya_ready, t + 1)
                        mean_square(Y[:, t, 0:512], 15 + t, 512)
                    for t in range(TILES):
                        name = ("cv", t)
                        filled_wait(act, name)
                        drain_inc(copy(XT[:, t, 0:4, :], quad(name)), name)
                    for t in range(TILES):
                        k = th[0]
                        th[0] += 1
                        act.wait_ge(gated, k - 1)
                        act.wait_ge(ln_done, t + 1)
                        av(TH[:, k % 2, :], XT[:, t, 0:4, :].rearrange("p a b -> p (a b)"), ACT.Tanh, scale=0.5).then_inc(v_tanh, 1)
                        if t:
                            act.wait_ge(yc_ready, t)
                            mean_square(Y[:, t - 1, 512:1024], 20 + t - 1, 512)
                    act.wait_ge(yc_ready, TILES)
                    mean_square(Y[:, TILES - 1, 512:1024], 20 + TILES - 1, 512)
                    for half, dst in ((0, OTOK), (1, VT)):
                        for t in range(TILES):
                            act.wait_ge(acc_filled[t], BLK["pe0"] + half + 1)
                            out = OTOK[:, t, :] if half == 0 else VT[:, 512 * t:512 * (t + 1)]
                            copy(out, acc[t][:, :]).then_inc(acc_drained[t], 1)
                    act.wait_ge(rstd_ready, 4)
                    for t in range(TILES):
                        copy(Y[:, t, 512:1024], Y[:, t, 512:1024], RS[:, 20 + t:21 + t]).then_inc(yc_scaled, 1)
                    for t in range(TILES):
                        act.wait_ge(acc_drained[t], BLK["o1"] + 1)
                        mean_square(H[:, t, :], 25 + t, D)
                    act.wait_ge(rstd_ready, 5)
                    for half in range(2):
                        for t in range(TILES):
                            act.wait_ge(acc_filled[t], BLK["pg0"] + half + 1)
                            tanh_acc(t, BLK["pg0"] + half, HR[:, t:t + 1])

                @block.vector
                def _(dve):
                    chain = Chain(dve, dve_chain)
                    tt, stt = nc.vector.tensor_tensor, nc.vector.scalar_tensor_tensor

                    def quad(name):
                        return bank(name)[:, :].rearrange("p (j t) -> p j t", t=P)

                    filled_wait(dve, "gain")
                    drain_inc(nc.vector.tensor_copy(GT[:, :], bank("gain")[:, 0:30]), "gain")
                    filled_wait(dve, "taps")
                    drain_inc(nc.vector.tensor_copy(CWT[:, :, :], bank("taps")[:, 0:4 * TAPS].rearrange("p (c k) -> p c k", c=4)), "taps")
                    copied_wait(dve, "gain")

                    def gained(name, col):
                        _, t, g = name
                        filled_wait(dve, name)
                        gains = GT[:, col + 4 * g:col + 4 * g + 4].unsqueeze(2).to_broadcast([P, 4, P])
                        drain_inc(tt(XT[:, t, 4 * g:4 * g + 4, :], quad(name), gains, ALU.mult), name)

                    for t in range(TILES):
                        for g in range(2):
                            gained(("x", t, g), G_IN)
                    dve.wait_ge(squares, 5)
                    chain.link(rsqrt(dve, chain, MS[:, 0:5], RS[:, 0:5], 5))
                    nc.vector.tensor_scalar(HR[:, 0:5], RS[:, 0:5], 0.5, None, ALU.mult).then_inc(rstd_ready, 1)

                    dve.wait_ge(squares, 15)
                    rsqrt(dve, chain, MS[:, 5:15], RS[:, 5:15], 10).then_inc(rstd_ready, 1)
                    dve.wait_ge(rstd_ready, 2)
                    dve.wait_ge(lnkv_in, 16)
                    for t in range(TILES):
                        lat = Z[:, t, QLORA:QLORA + LORA]
                        stt(out=lat, in0=lat, scalar=RS[:, 10 + t:11 + t], in1=LNKV[:, :], op0=ALU.mult, op1=ALU.mult)
                    kr = Z[:, :, NZ - ROPE:NZ].rearrange("p t (a e) -> p t a e", a=2)
                    tt(KRA[:, :, :, :], kr, ROPEK[:, :, 0:2, :], ALU.mult)
                    tt(KRB[:, :, 0, :], kr[:, :, 1, :], ROPEK[:, :, 2, :], ALU.mult)
                    chain.link(tt(KRB[:, :, 1, :], kr[:, :, 0, :], ROPEK[:, :, 3, :], ALU.mult))
                    kr2 = Z[:, :, NZ:NZ + ROPE].rearrange("p t (a e) -> p t a e", a=2)
                    tt(kr2, KRA[:, :, :, :], KRB[:, :, :, :], ALU.add)
                    tt(kr, KRA[:, :, :, :], KRB[:, :, :, :], ALU.add).then_inc(latents_ready, 1)

                    k_th = [0]

                    def gate(out, other, ready, value):
                        k = k_th[0]
                        k_th[0] += 1
                        dve.wait_ge(ready, value)
                        return stt(out=out, in0=TH[:, k % 2, :], scalar=1.0, in1=other, op0=ALU.add, op1=ALU.mult)

                    for t in range(TILES):
                        u = Y[:, t, 512:1024]
                        gate(u, u, acc_drained[t], BLK["ug"] + 1).then_inc(gated, 1)
                    for g in range(2):
                        name = f"qs{g}"
                        filled_wait(dve, name)
                        rope = ROPET[:, SEQ:TOK].rearrange("p (s t) -> p s t", t=NS)
                        for j in range(4):
                            last = tt(QS[:, :, 4 * g + j, :], quad(name)[:, j, :].rearrange("p (s t) -> p s t", t=NS),
                                      rope, ALU.mult)
                        drain_inc(last, name)

                    def tap(k):
                        n = 8 * k
                        for c in range(4):
                            w = CWT[:, c, k:k + 1]
                            bias = GT[:, G_CB + c:G_CB + c + 1]
                            for part in range(2):
                                if part == 0:
                                    out, src = VTv[:, c, 0:SEQ], UT[:, c, k:k + SEQ]
                                else:
                                    out = VTv[:, c, SEQ:TOK].rearrange("p (b j) -> p b j", b=NB)
                                    src = UTS[:, c, :, k:k + NS]
                                if k == 0:
                                    ins = nc.vector.tensor_scalar(out, src, w, bias, ALU.mult, ALU.add)
                                else:
                                    dve.wait_ge(conv_done, n - 7)
                                    ins = stt(out=out, in0=src, scalar=w, in1=out, op0=ALU.mult, op1=ALU.add)
                                ins.then_inc(conv_done, 1)
                                n += 1

                    def mask(n, w, add):
                        name = ("s", n)
                        filled_wait(dve, name)
                        drain_inc(nc.vector.tensor_tensor_reduce(SB[:, n % 2, 0:w], bank(name)[:, 0:w], add, -SCALE, 3e38,
                                                                 ALU.add, ALU.min, NBIAS[:, n:n + 1]), name)

                    def filler_gate(q):
                        name, q = ("ga", q) if q < 10 else ("gc", q - 10)
                        if q < 5:
                            return
                        t = q - 5
                        col = 0 if name == "ga" else 512
                        y = Y[:, t, col:col + 512]
                        gate(y, y, acc_drained[t], BLK[name] + 1).then_inc(gated, 1)

                    for t in range(TILES):
                        copied_wait(dve, ("u", t))
                    for s in range(NB):
                        mask(s, PAST + P, MASK[:, 0:PAST + P])
                        for k in TAP_S.get(s, []):
                            tap(k)
                        dve.wait_ge(exped, s + 1)
                        chain.link(nc.vector.reciprocal(RSUM[:, s:s + 1], SUMS[:, s:s + 1]))
                        nc.vector.tensor_scalar(SB[:, s % 2, 0:PAST + P], SB[:, s % 2, 0:PAST + P],
                                                RSUM[:, s:s + 1], None, ALU.mult).then_inc(p_scaled, 1)
                        filler_gate(FILL_S[s])

                    def queries_out(h):
                        name = ("q", h)
                        filled_wait(dve, name)
                        drain_inc(tt(QH[:, h % 2, :], bank(name)[:, :], ROPET[:, 0:SEQ], ALU.mult), name)

                    def head_out(h):
                        name = ("oh", h)
                        n = NB + 4 * h
                        dve.wait_ge(exped, n + 4)
                        chain.link(nc.vector.reciprocal(RSUM[:, n:n + 4], SUMS[:, n:n + 4]))
                        filled_wait(dve, name)
                        own = quad(name)[:, :, VH * (h % 2):VH * (h % 2 + 1)]
                        drain_inc(tt(OTOK[:, 0:4, VH * h:VH * (h + 1)], own,
                                     RSUM[:, n:n + 4].unsqueeze(2).to_broadcast([P, 4, VH]), ALU.mult), name)

                    queries_out(0)
                    mask(NB, P, MASK[:, 512 - P:512])
                    for u in range(UNITS):
                        h, i = divmod(u, 4)
                        if u < UNITS - 1:
                            w = P * ((i + 1) % 4 + 1)
                            mask(NB + u + 1, w, MASK[:, 512 - w:512])
                        if i == 0 and h:
                            head_out(h - 1)
                        if i == 2 and h < HEADS - 1:
                            queries_out(h + 1)
                        for k in TAP_P.get(u, []):
                            tap(k)
                        if u in FILL_P:
                            filler_gate(FILL_P[u])
                    head_out(HEADS - 1)
                    copied_wait(dve, ("oh", HEADS - 1))
                    copied_wait(dve, "oa")
                    dve.wait_ge(gated, 15)
                    for t in range(TILES):
                        y = Y[:, t, 0:512]
                        tt(y, y, OTOK[:, t, :], ALU.mult).then_inc(ya_ready, 1)

                    for t in range(TILES):
                        copied_wait(dve, ("cv", t))
                        last = nc.vector.bn_stats(BN6[:, t, :], XT[:, t, 0:4, :].rearrange("p a b -> p (a b)"))
                    chain.link(last)
                    for t in range(TILES):
                        last = nc.vector.bn_aggr(MV[:, t, :], BN6[:, t, :])
                    chain.link(last)
                    rsqrt(dve, chain, MV[:, :, 1], RSV[:, :], TILES).then_inc(rstd_ready, 1)
                    dve.wait_ge(rstd_ready, 3)
                    dve.wait_ge(lnconv_in, 32)
                    for t in range(TILES):
                        v = XT[:, t, 0:4, :].rearrange("p a b -> p (a b)")
                        chain.link(nc.vector.tensor_scalar(v, v, MV[:, t, 0:1], RSV[:, t:t + 1], ALU.subtract, ALU.mult))
                        tt(v, v, LCG[:, :], ALU.mult).then_inc(ln_scaled, 1)
                    for t in range(TILES):
                        v = XT[:, t, 0:4, :].rearrange("p a b -> p (a b)")
                        gate(v, v, v_tanh, t + 1).then_inc(gated, 1)
                        dve.wait_ge(gated, 16 + t)
                        y = Y[:, t, 512:1024]
                        stt(out=y, in0=v, scalar=0.5, in1=y, op0=ALU.mult, op1=ALU.mult).then_inc(yc_ready, 1)
                    dve.wait_ge(squares, 25)
                    rsqrt(dve, chain, MS[:, 15:25], RS[:, 15:25], 10).then_inc(rstd_ready, 1)
                    dve.wait_ge(rstd_ready, 4)
                    for t in range(TILES):
                        y = Y[:, t, 0:512]
                        nc.vector.tensor_scalar(y, y, RS[:, 15 + t:16 + t], None, ALU.mult).then_inc(ya_scaled, 1)
                    for t in range(TILES):
                        for g in range(2):
                            gained(("y", t, g), G_OUT)
                    for half in range(2):
                        for t in range(TILES):
                            dve.wait_ge(acc_filled[t], BLK["o0"] + half + 1)
                            hh = H[:, t, 512 * half:512 * (half + 1)]
                            tt(hh, hh, acc[t][:, :], ALU.add).then_inc(acc_drained[t], 1)
                            if half and t > 2:
                                for g in range(2):
                                    gained(("h", t - 3, g), G_PG)
                    for t in range(TILES - 3, TILES):
                        for g in range(2):
                            gained(("h", t, g), G_PG)
                    dve.wait_ge(squares, 30)
                    chain.link(rsqrt(dve, chain, MS[:, 25:30], RS[:, 25:30], 5))
                    nc.vector.tensor_scalar(HR[:, 0:5], RS[:, 25:30], 0.5, None, ALU.mult).then_inc(rstd_ready, 1)
                    for half in range(2):
                        for t in range(TILES):
                            emb = OTOK[:, t, :] if half == 0 else VT[:, 512 * t:512 * (t + 1)]
                            gate(emb, emb, acc_drained[t], BLK["pg0"] + half + 1).then_inc(gated, 1)
                            dve.wait_ge(gated, 21 + 5 * half + t)
                            hh = H[:, t, 512 * half:512 * (half + 1)]
                            stt(out=hh, in0=emb, scalar=0.5, in1=hh, op0=ALU.mult, op1=ALU.add).then_inc(h_done, 1)

                @block.gpsimd
                def _(pool):
                    def load_cache(s):
                        src = a["cache_ckv"][bass.ds(layer, 1), s]
                        pool.dma_start(CKV[:, s % 2, :, :], src.rearrange("o (j p) r -> p (o j) r", p=P)).then_inc(cache_in[s % 2], 16)
                        src = a["cache_krope"][bass.ds(layer, 1), s].rearrange("o (j p) r -> p (o j) r", p=P)
                        for k in range(2):
                            lo = NOPE + ROPE * k
                            pool.dma_start(CKR[:, s % 2, :, lo:lo + ROPE], src).then_inc(cache_in[s % 2], 16)

                    load_cache(0)
                    load_cache(1)
                    pool.dma_start(a["new_conv_sample"][bass.ds(layer, 1), :, 0:STATE - NS, :],
                                   a["state_conv"][bass.ds(layer, 1), :, NS:STATE, :]).then_inc(states_stored, 16)
                    pool.wait_ge(latents_ready, 1)
                    for name, rows, col, n in (("new_ckv", None, QLORA, LORA), ("new_krope", None, NZ - ROPE, ROPE)):
                        pool.dma_start(at(name + "_prompt").rearrange("l o (t p) r -> p (l o t) r", p=P),
                                       Z[:, 0:4, col:col + n]).then_inc(latents_stored, 16)
                        pool.dma_start(at(name + "_sample").rearrange("o b s r -> (o b s) r"),
                                       Z[:, 4, col:col + n]).then_inc(latents_stored, 16)
                    pool.wait_ge(gated, TILES)
                    pool.dma_start(at("new_conv_prompt").rearrange("l o s c -> (l o s) c"),
                                   Y[P - STATE:P, TILES - 2, 512:1024]).then_inc(u_stored, 16)
                    for s in range(NB):
                        pool.dma_start(a["new_conv_sample"][bass.ds(layer, 1), s, STATE - NS:STATE, :].rearrange("o s c -> (o s) c"),
                                       Y[NS * s:NS * (s + 1), TILES - 1, 512:1024]).then_inc(u_stored, 16)
                    for s in range(2, NB):
                        filled_wait(pool, ("o", s - 2))
                        load_cache(s)
                    pool.wait_ge(lnconv_in, 32)
                    for t in range(TILES):
                        pool.wait_ge(ln_scaled, t + 1)
                        v = XT[:, t, 0:4, :].rearrange("p a b -> p (a b)")
                        nc.gpsimd.tensor_tensor(v, v, LCB[:, :], ALU.add).then_inc(ln_done, 1)
                    pool.wait_ge(latents_stored, 64)
                    pool.wait_ge(u_stored, 16 * (1 + NB))
                    pool.wait_ge(states_stored, 16)

            nc.gpsimd.dma_reset(range(sems[0].num, sems[-1].num + 1))
            nc.gpsimd.sem_clear(range(sems[0].num, sems[-1].num + 1))
            nc.all_engine_barrier()

        LNF = WR[:, 0, 0:D]
        OUT = XT[:, :, :, :].rearrange("p t k n -> p t (k n)")
        with nc.Block() as block:
            @block.sync
            def _(sp):
                sp.dma_start(LNF, a["ln_f"].unsqueeze(0).to_broadcast([P, D])).then_inc(const_in, 16)
                for t in range(TILES):
                    sp.wait_ge(h_done, t + 1)
                    dst = a["y_prompt"][0, P * t:P * (t + 1), :] if t < 4 else a["y_sample"].rearrange("b s d -> (b s) d")
                    sp.dma_start(dst, OUT[:, t, :]).then_inc(y_stored, 16)
                sp.wait_ge(y_stored, 16 * TILES)

            @block.scalar
            def _(act):
                for t in range(TILES):
                    if t:
                        act.wait_ge(squares, t)
                    nc.scalar.activation(JUNK[:, :], H[:, t, :], ACT.Square, scale=D ** -0.5,
                                         accum_out=MS[:, t:t + 1]).then_inc(squares, 1)

            @block.vector
            def _(dve):
                chain = Chain(dve, dve_chain)
                dve.wait_ge(squares, TILES)
                chain.link(rsqrt(dve, chain, MS[:, 0:5], RS[:, 0:5], 5))
                dve.wait_ge(const_in, 16)
                for t in range(TILES):
                    nc.vector.scalar_tensor_tensor(out=OUT[:, t, :], in0=H[:, t, :], scalar=RS[:, t:t + 1], in1=LNF,
                                                   op0=ALU.mult, op1=ALU.mult).then_inc(h_done, 1)


_INS = ["x_prompt", "x_sample", "cache_ckv", "cache_krope", "state_conv", "p_prompt", "p_sample", "ln_in", "w_in",
        "ln_q", "w_q_b", "ln_kv", "w_kv_b", "conv_w", "conv_b", "ln_conv_g", "ln_conv_b", "ln_out_a", "ln_out_c",
        "w_out", "w_pe", "ln_pg", "w_pg", "ln_f"]
_OUTS = [("y_prompt", (1, SEQ, D)), ("y_sample", (NB, NS, D)),
         ("new_ckv_prompt", (DEPTH, 1, SEQ, LORA)), ("new_krope_prompt", (DEPTH, 1, SEQ, ROPE)),
         ("new_conv_prompt", (DEPTH, 1, STATE, CH)),
         ("new_ckv_sample", (DEPTH, NB, NS, LORA)), ("new_krope_sample", (DEPTH, NB, NS, ROPE)),
         ("new_conv_sample", (DEPTH, NB, STATE, CH))]


def constants():
    import numpy as np
    f = np.float32
    half = ROPE // 2
    inv = (f(10000.0) ** (-np.arange(half, dtype=f) / f(half))).astype(f)
    pos = np.concatenate([np.arange(SEQ), np.tile(PAST + np.arange(NS), NB)]).astype(f)
    ang = pos[:, None] * inv[None, :]
    cos, sin = np.cos(ang).astype(f), np.sin(ang).astype(f)
    ropet = np.ones((P, TOK), f)
    ropet[64:80] = cos.T
    ropet[80:96] = cos.T
    ropet[96:112] = -sin.T
    ropet[112:128] = sin.T
    ropek = np.stack([cos, cos, -sin, sin], axis=1).reshape(TILES, P, 4, half).transpose(1, 0, 2, 3)
    mask = np.zeros((P, 512), f)
    mask[0:64, 448:512] = NEG
    mrow = np.full((1, 240), NEG, f)
    mrow[0, 112:128] = 0.0
    return {"c_ident": np.eye(P, dtype=f), "c_ropet": ropet, "c_ropek": np.ascontiguousarray(ropek),
            "c_mask": mask, "c_mrow": mrow}


def kernel(**inputs):
    import numpy as _np
    import concourse.bacc as _bacc
    from concourse import mybir as _mybir
    from concourse.bass_utils import run_bass_kernel_spmd as _run

    nc = _bacc.Bacc("TRN2", target_bir_lowering=False, num_devices=1)
    given = {name: _np.ascontiguousarray(inputs[name]) for name in _INS}
    given.update(constants())
    arrays, aps = {}, {}
    for name, x in given.items():
        arrays[f"in_{name}_dram"] = x
        aps[name] = nc.dram_tensor(f"in_{name}_dram", x.shape, _mybir.dt.from_np(x.dtype), kind="ExternalInput").ap()
    for name, shape in _OUTS:
        aps[name] = nc.dram_tensor(f"out_{name}_dram", shape, F32, kind="ExternalOutput").ap()
    build(nc, aps)
    r = _run(nc, [arrays], core_ids=[0])
    return tuple(r.results[0][f"out_{name}_dram"] for name, _ in _OUTS)
```

```python
from contextlib import ExitStack

import concourse.bass as bass
from concourse import mybir

ALU = mybir.AluOpType
ACT = mybir.ActivationFunctionType
F32 = mybir.dt.float32
F32R = mybir.dt.float32r
I32 = mybir.dt.int32
BF16 = mybir.dt.bfloat16

P = 128
D = 1024
SEQ = 512
DEPTH = 2
NB, NS, PAST = 8, 16, 256
PLE = 256
HEADS, NOPE, ROPE, VH = 8, 64, 32, 64
LORA, QLORA = 128, 256
CH, TAPS = 512, 31
STATE = TAPS - 1
SCALE = float(NOPE + ROPE) ** -0.5
EPS = 1e-6
NEG = -1e30
TILES = SEQ // P + 1
TOK = TILES * P
KT = D // P
RAW = 3
SPLIT = 2
CACHED = 4
NZ = QLORA + LORA + ROPE
MAGIC = float(0x5F3759DF)

BLOCKS = ["uv", "ug", "zA", "gc", "ga", "pe0", "pe1", "o0", "o1", "pg0", "pg1"]
BLK = {name: i for i, name in enumerate(BLOCKS)}
ZCOL = {"zA": (0, NZ), "ga": (NZ, 512), "uv": (NZ + 512, 512), "ug": (NZ + 1024, 512), "gc": (NZ + 1536, 512)}


CHUNKS = [(b, c) for b in BLOCKS for c in ((0,) if b[:2] == "pe" else range(4))]
PARTS = [c for c in CHUNKS if c[0][:2] != "pe"]
PART = {c: i for i, c in enumerate(PARTS)}
UNITS = HEADS * (SEQ // P)
QUANTA = [(b, c, t) for b in ("gc", "ga") for c in range(4) for t in range(TILES)]
EARLY = 2 * TILES
FILL = {}
for _q in range(EARLY, len(QUANTA)):
    FILL[_q - EARLY] = _q
_taps = list(range(TAPS))


def _next_taps(n):
    out, _taps[:n] = _taps[:n], []
    return out


TAP = {name: _next_taps(n) for name, n in (("early", 5), ("latents", 1), ("queries", 1))}
for _n in range(NB):
    TAP[_n] = _next_taps(1)
TAP["turn"] = _next_taps(2)
for _u in range(UNITS):
    TAP[NB + _u] = _next_taps(0 if _u % 3 == 2 else 1)
EMBED = UNITS - 8
V_EARLY = 2
CONV_OUT = NB + 23
NORMED = NB + UNITS - (CONV_OUT + TILES)


def shared_bank_plan():
    order = {"S": [], "T": [], "O": []}
    turn = [0]

    def cyc(*names):
        for n in names:
            order["STO"[turn[0] % 3]].append(n)
            turn[0] += 1

    cyc("gain", "taps")
    for t in range(TILES):
        for g in range(2):
            cyc(("x", t, g))
    cyc("uk0", "uk1", "st0", "st1", "p0", "p1", "p2")
    for t in range(TILES):
        cyc(("u", t))
    for t in range(TILES):
        cyc(("small", t))
    cyc("qs0", "qs1", "ql0", "ql1")
    order["T"] += [("c", 0), ("c", 1)]
    for s in range(NB):
        order["S"].append(("s", s))
        order["O"].append(("o", s))
        if s < NB - 2:
            order["T"].append(("c", s + 2))
        order["T"].append(("p", s))
    order["T"] += [("k", 0), ("q", 0)]
    for j in range(4):
        cyc(("v", j))
    order["S"].append("oa")
    for u in range(UNITS):
        h, i = divmod(u, 4)
        order["S"].append(("s", NB + u))
        if i == 0:
            order["O"].append(("oh", h))
        if i == 1 and h < HEADS - 1:
            order["T"].append(("k", h + 1))
        if i == 2 and h < HEADS - 1:
            order["T"].append(("q", h + 1))
        if 0 <= NB + u - CONV_OUT < TILES:
            order["T"].append(("cv", NB + u - CONV_OUT))
        order["T"].append(("p", NB + u))
    for g in range(2):
        for t in range(TILES):
            cyc(("y", t, g))
    for t in range(TILES):
        for g in range(2):
            cyc(("h", t, g))
    return {n: (b, i) for b, names in order.items() for i, n in enumerate(names)}


def build(nc, a):
    ctx = ExitStack()
    plan = shared_bank_plan()
    with ctx:
        def sb(name, shape, dt=F32):
            return ctx.enter_context(nc.sbuf_tensor(name, shape, dt))

        H = sb("H", [P, TILES, D])
        Y = H
        XHI = sb("XHI", [P, TILES, KT, P], F32R)
        XLO = sb("XLO", [P, TILES, KT, P], F32R)
        WR = sb("WR", [P, RAW, 2, 512])
        WHI = sb("WHI", [P, SPLIT, 2, 512], F32R)
        WLO = sb("WLO", [P, SPLIT, 2, 512], F32R)
        OTOK = sb("OTOK", [P, TILES, 512])
        PTR = sb("PTR", [P, 2, TOK])
        UT = sb("UT", [P, 4, STATE + SEQ])
        UTS = sb("UTS", [P, 4, NB, STATE + NS])
        VT = sb("VT", [P, 4 * TOK])
        VTv = VT[:, :].rearrange("p (t c e) -> p t c e", c=4, e=P)
        EMB = [[UT[:, t, STATE:] for t in range(TILES - 1)], []]
        WQ = sb("WQ", [P, 2, HEADS, 128])
        WKV = sb("WKV", [P, HEADS, 128])
        Z = sb("Z", [P, TILES, NZ + ROPE])
        CQT = sb("CQT", [P, 2, TOK])
        CKVT = sb("CKVT", [P, TOK])
        KRS = sb("KRS", [P, P])
        V = sb("V", [P, 4, 512])
        QL = V[:, 0:2, :].rearrange("p a (s h t) -> p (a s) h t", h=HEADS, t=NS)
        OL = sb("OL", [P, HEADS, P])
        UKT = OL
        EMB[0].append(UTS[:, :, :, :].rearrange("p c b j -> p (c b j)")[:, 0:512])
        EMB[1] += [OTOK[:, t, :] for t in range(TILES)]
        KH = sb("KH", [P, 2, 512])
        QH = sb("QH", [P, 2, 512])
        QS = QH[:, :, :].rearrange("p a (s h t) -> p (a s) h t", h=HEADS, t=NS)
        SB = sb("SB", [P, 2, 512])
        PT = sb("PT", [P, 2, 4, P])
        CKV = V[:, 2:4, :].rearrange("p a (b j r) -> p (a b) j r", b=2, r=LORA)
        CKR = sb("CKR", [P, CACHED, 2, 128])
        CTK = sb("CTK", [P, 512])
        TH = sb("TH", [P, 2, 512])
        ROWS = VT[0:30, 1536:1536 + P]
        GT = sb("GT", [P, 30])
        CWT = sb("CWT", [P, 4, TAPS])
        LNKV = sb("LNKV", [P, LORA])
        LCG = sb("LCG", [P, CH])[:, :]
        LCB = CTK[:, :]
        IDENT = sb("IDENT", [P, P])
        ROPET = sb("ROPET", [P, TOK])
        ROPEK = sb("ROPEK", [P, TILES, 4, 16])
        MASK = sb("MASK", [P, 512], BF16)
        MROW = sb("MROW", [1, 240])
        ONES = sb("ONES", [1, P])
        JUNK = sb("JUNK", [P, D], BF16)
        MS = sb("MS", [P, 32])
        RS = sb("RS", [P, 32])
        HR = sb("HR", [P, 8])
        NR = sb("NR", [P, 3, 16])
        RSV = sb("RSV", [P, TILES])
        KRA = SB[:, 0, 0:32 * TILES].rearrange("p (t a e) -> p t a e", t=TILES, a=2)
        KRB = SB[:, 1, 0:32 * TILES].rearrange("p (t a e) -> p t a e", t=TILES, a=2)
        NBIAS = sb("NBIAS", [P, NB + UNITS])
        SUMS = sb("SUMS", [P, NB + UNITS])
        RSUM = sb("RSUM", [P, NB + UNITS])
        BN6 = sb("BN6", [P, TILES, 6])
        MV = sb("MV", [P, TILES, 2])

        G_IN, G_PG, G_OUT, G_Q, G_CB = 0, 8, 16, 24, 26

        acc = [ctx.enter_context(nc.psum_tensor(f"acc{t}", [P, 512], F32)) for t in range(TILES)]
        shared = {b: ctx.enter_context(nc.psum_tensor(f"shared{b}", [P, 512], F32)) for b in "STO"}

        sems = []

        def sem(name):
            s = ctx.enter_context(nc.semaphore(name))
            sems.append(s)
            return s

        filled = {b: sem(f"filled_{b}") for b in "STO"}
        drained = {b: sem(f"drained_{b}") for b in "STO"}
        acc_filled = [sem(f"acc_filled{t}") for t in range(TILES)]
        acc_drained = [sem(f"acc_drained{t}") for t in range(TILES)]
        w_loaded = [sem(f"w_loaded{i}") for i in range(RAW)]
        hi_ready = sem("hi_ready")
        split_ready = sem("split_ready")
        piece_used = sem("piece_used")
        half_hi = sem("half_hi")
        spilled = sem("spilled")
        h_in = [sem(f"h_in{half}") for half in range(2)]
        rows_in = sem("rows_in")
        taps_in = sem("taps_in")
        state_in = sem("state_in")
        p_in = sem("p_in")
        wq_in = sem("wq_in")
        wq_rot = sem("wq_rot")
        wkv_in = sem("wkv_in")
        lnkv_in = sem("lnkv_in")
        lnconv_in = sem("lnconv_in")
        cache_in = [sem(f"cache_in{i}") for i in range(CACHED)]
        squares = sem("squares")
        rstd_ready = sem("rstd_ready")
        cq_scaled = sem("cq_scaled")
        latents_ready = sem("latents_ready")
        gated = sem("gated")
        exped = sem("exped")
        p_scaled = sem("p_scaled")
        conv_done = sem("conv_done")
        ln_scaled = sem("ln_scaled")
        ln_done = sem("ln_done")
        stats_ready = sem("stats_ready")
        v_tanh = sem("v_tanh")
        ya_ready = sem("ya_ready")
        yc_ready = sem("yc_ready")
        ya_scaled = sem("ya_scaled")
        yc_scaled = sem("yc_scaled")
        h_done = sem("h_done")
        latents_stored = sem("latents_stored")
        u_stored = sem("u_stored")
        states_stored = sem("states_stored")
        dve_chain = sem("dve_chain")
        act_chain = sem("act_chain")
        const_in = sem("const_in")
        const_set = sem("const_set")
        y_stored = sem("y_stored")

        def bank(name):
            return shared[plan[name][0]]

        def fill_wait(eng, name):
            b, i = plan[name]
            if i:
                eng.wait_ge(drained[b], i)

        def fill_inc(ins, name):
            ins.then_inc(filled[plan[name][0]], 1)

        def filled_wait(eng, name):
            b, i = plan[name]
            eng.wait_ge(filled[b], i + 1)

        def drain_inc(ins, name):
            ins.then_inc(drained[plan[name][0]], 1)

        def copied_wait(eng, name):
            b, i = plan[name]
            eng.wait_ge(drained[b], i + 1)

        class Chain:

            def __init__(self, eng, s):
                self.eng, self.s, self.n = eng, s, 0

            def link(self, ins):
                self.n += 1
                ins.then_inc(self.s, 1)
                self.eng.wait_ge(self.s, self.n)

        def rsqrt(eng, chain, src, dst, n):
            half = NR[:, 0, 0:n]
            tmp = NR[:, 1, 0:n]
            x = NR[:, 2, 0:n]
            chain.link(eng.tensor_scalar(x, src, EPS, None, ALU.add))
            chain.link(eng.tensor_scalar(half, x, -0.5, None, ALU.mult))
            chain.link(eng.tensor_scalar(dst.bitcast(I32), x.bitcast(I32), -0.5, MAGIC, ALU.mult, ALU.add))
            for k in range(3):
                chain.link(eng.tensor_tensor(tmp, dst, dst, ALU.mult))
                chain.link(eng.tensor_tensor(tmp, tmp, half, ALU.mult))
                last = eng.scalar_tensor_tensor(out=dst, in0=tmp, scalar=1.5, in1=dst, op0=ALU.add, op1=ALU.mult)
                if k < 2:
                    chain.link(last)
            return last

        def part_used(eng, i):
            name, c = PARTS[i]
            if c == 3:
                eng.wait_ge(acc_filled[TILES - 1], BLK[name] + 1)
            else:
                eng.wait_ge(piece_used, sum(x != 3 for _, x in PARTS[:i + 1]))

        def gain_column(i, k):
            name, c = PARTS[i]
            col = G_IN if name in ZCOL else G_OUT if name[0] == "o" else G_PG
            return GT[:, col + 2 * c + k:col + 2 * c + k + 1]

        def width(name):
            return NZ if name == "zA" else 512

        def raw_slot(i):
            j = CHUNKS.index(PARTS[i])
            return j, WR[:, j % RAW, :, 0:width(PARTS[i][0])]

        spill = nc.dram_tensor("residual_spill", (P, TILES, D), F32, kind="Internal").ap()

        with nc.Block() as block:
            @block.sync
            def _(sp):
                sp.dma_start(H[:, 0:4, :], a["x_prompt"].rearrange("o (t p) d -> p (o t) d", p=P)).then_inc(const_in, 16)
                sp.dma_start(H[:, 4, :], a["x_sample"].rearrange("b s d -> (b s) d")).then_inc(const_in, 16)
                sp.dma_start(IDENT[:, :], a["c_ident"]).then_inc(const_in, 16)
                sp.dma_start(ROPET[:, :], a["c_ropet"]).then_inc(const_in, 16)
                sp.dma_start(ROPEK[:, :, :, :], a["c_ropek"]).then_inc(const_in, 16)
                sp.dma_start(MROW[:, :], a["c_mrow"]).then_inc(const_in, 16)
                sp.wait_ge(const_in, 16 * 6)

            @block.gpsimd
            def _(pool):
                nc.gpsimd.memset(UT[:, :, 0:STATE], 0.0).then_inc(const_set, 1)
                nc.gpsimd.memset(CKR[:, :, :, 0:NOPE], 0.0).then_inc(const_set, 1)
                nc.gpsimd.memset(ONES[:, :], 1.0).then_inc(const_set, 1)
                nc.gpsimd.memset(MASK[:, :], 0.0).then_inc(const_set, 1)
                pool.wait_ge(const_set, 4)
                nc.gpsimd.memset(MASK[0:P // 2, 512 - P // 2:512], NEG).then_inc(const_set, 1)

        with nc.Fori(0, DEPTH) as layer:
            def at(name):
                return a[name][bass.ds(layer, 1)]

            with nc.Block() as block:
                @block.sync
                def _(sp):
                    for name, g, n in (("ln_in", G_IN, 8), ("ln_pg", G_PG, 8), ("ln_out_a", G_OUT, 4),
                                       ("ln_out_c", G_OUT + 4, 4), ("ln_q", G_Q, 2), ("conv_b", G_CB, 4)):
                        sp.dma_start(ROWS[g:g + n, :], at(name).rearrange("o (k p) -> (o k) p", p=P)).then_inc(rows_in, 16)

                    def chunk(j):
                        name, c = CHUNKS[j]
                        if j >= RAW:
                            before = CHUNKS[j - RAW]
                            if before in PART:
                                sp.wait_ge(split_ready, PART[before] + 1)
                            else:
                                sp.wait_ge(acc_filled[TILES - 1], BLK[before[0]] + 1)
                        if name in ZCOL:
                            w, (col, n) = "w_in", ZCOL[name]
                        else:
                            w, col, n = {"o": "w_out", "e": "w_pe", "g": "w_pg"}[name[-2]], 512 * int(name[-1]), 512
                        src = at(w)[:, 2 * P * c:2 * P * (c + 1), col:col + n]
                        sp.dma_start(WR[:, j % RAW, :, 0:n],
                                     src.rearrange("o (k p) n -> p (o k) n", p=P)).then_inc(w_loaded[j % RAW], 16)

                    chunk(0)
                    chunk(1)
                    sp.dma_start(VT[0:TAPS, 1024:1536], at("conv_w").rearrange("o k c -> (o k) c")).then_inc(taps_in, 16)
                    sp.dma_start(WKV[:, :, :], at("w_kv_b").rearrange("o r (h e) -> (o r) h e", e=128)).then_inc(wkv_in, 16)
                    sp.dma_start(VT[0:120, 0:1024].rearrange("p (a c) -> p a c", a=2),
                                 at("state_conv").rearrange("o (a b) j c -> (b j) (o a) c", a=2)).then_inc(state_in, 16)
                    sp.dma_start(OTOK[:, 0:4, 0:PLE], at("p_prompt").rearrange("l o (t p) d -> p (l o t) d", p=P)).then_inc(p_in, 16)
                    sp.dma_start(OTOK[:, 4, 0:PLE], at("p_sample").rearrange("o b s d -> (o b s) d")).then_inc(p_in, 16)
                    chunk(2)
                    for k in range(2):
                        sp.dma_start(WQ[:, k, :, 0:NOPE + ROPE],
                                     at("w_q_b")[:, P * k:P * (k + 1), :].rearrange("o p (h e) -> (o p) h e", h=HEADS)).then_inc(wq_in, 16)
                    sp.dma_start(LNKV[:, :], at("ln_kv").to_broadcast([P, LORA])).then_inc(lnkv_in, 16)
                    sp.dma_start(spill, H[:, :, :]).then_inc(spilled, 16)
                    back = CHUNKS.index(("o0", 3)) + 1
                    for j in range(3, back):
                        chunk(j)
                    sp.wait_ge(spilled, 16)
                    for half in range(2):
                        cols = slice(512 * half, 512 * (half + 1))
                        for t in range(TILES):
                            filled_wait(sp, ("y", t, half))
                            sp.dma_start(H[:, t, cols], spill[:, t, cols]).then_inc(h_in[half], 16)
                        if half == 0:
                            chunk(back)
                            back += 1
                    for j in range(back, len(CHUNKS)):
                        chunk(j)

                @block.tensor
                def _(pe):
                    mm = nc.tensor.matmul

                    def flip(out, in_):
                        rows = in_.shape[0]
                        return nc.tensor.transpose(out, in_, IDENT[0:rows, 0:rows])

                    def quad(name):
                        return bank(name)[:, :].rearrange("p (j t) -> p j t", t=P)

                    fill_wait(pe, "gain")
                    pe.wait_ge(rows_in, 16 * 6)
                    fill_inc(flip(bank("gain")[:, 0:30], ROWS[:, :]), "gain")
                    fill_wait(pe, "taps")
                    pe.wait_ge(taps_in, 16)
                    for c in range(4):
                        last = flip(bank("taps")[:, TAPS * c:TAPS * (c + 1)], VT[0:TAPS, 1024 + P * c:1024 + P * (c + 1)])
                    fill_inc(last, "taps")

                    def flip_half(name, src):
                        g = name[2]
                        fill_wait(pe, name)
                        for j in range(4):
                            last = flip(quad(name)[:, j, :], src[:, P * (4 * g + j):P * (4 * g + j + 1)])
                        fill_inc(last, name)

                    for t in range(TILES):
                        for g in range(2):
                            flip_half(("x", t, g), H[:, t, :])
                    def turn_small():
                        pe.wait_ge(wkv_in, 16)
                        for g in range(2):
                            name = f"uk{g}"
                            fill_wait(pe, name)
                            for j in range(4):
                                last = flip(quad(name)[0:NOPE, j, :], WKV[:, 4 * g + j, 0:NOPE])
                            fill_inc(last, name)
                        pe.wait_ge(state_in, 16)
                        for g in range(2):
                            name = f"st{g}"
                            fill_wait(pe, name)
                            for c in range(4):
                                last = flip(bank(name)[:, 120 * c:120 * (c + 1)], VT[0:120, 512 * g + P * c:512 * g + P * (c + 1)])
                            fill_inc(last, name)

                    def turn_embeddings():
                        pe.wait_ge(p_in, 32)
                        for g in range(3):
                            name = f"p{g}"
                            fill_wait(pe, name)
                            for j, t in enumerate(range(2 * g, min(2 * g + 2, TILES))):
                                for k in range(2):
                                    last = flip(quad(name)[:, 2 * j + k, :], OTOK[:, t, P * k:P * (k + 1)])
                            fill_inc(last, name)

                    def quantum(name, c, t):
                        i = PART[(name, c)]
                        n = width(name)
                        first, final = c == 0, c == 3
                        if t == 0:
                            pe.wait_ge(split_ready, i + 1)
                        if first and BLK[name]:
                            pe.wait_ge(acc_drained[t], BLK[name])
                        for k in range(2):
                            hi, lo = XHI[:, t, 2 * c + k, :], XLO[:, t, 2 * c + k, :]
                            w_hi, w_lo = WHI[:, i % SPLIT, k, 0:n], WLO[:, i % SPLIT, k, 0:n]
                            out = acc[t][:, 0:n]
                            mm(out, hi, w_hi, start=(first and k == 0), stop=False)
                            mm(out, hi, w_lo, start=False, stop=False)
                            last = mm(out, lo, w_hi, start=False, stop=(final and k == 1))
                        if final:
                            last.then_inc(acc_filled[t], 1)
                        elif t == TILES - 1:
                            last.then_inc(piece_used, 1)

                    for name in ("uv", "ug"):
                        for c in range(4):
                            for t in range(TILES):
                                if name == "uv":
                                    copied_wait(pe, ("x", t, c // 2))
                                quantum(name, c, t)
                            if name == "uv" and c == 0:
                                turn_small()
                            if name == "uv" and c == 1:
                                turn_embeddings()
                    for c in range(4):
                        if c == 2:
                            for t in range(TILES):
                                name = ("u", t)
                                fill_wait(pe, name)
                                pe.wait_ge(gated, t + 1)
                                for b in range(4):
                                    last = flip(quad(name)[:, b, :], Y[:, t, 512 + P * b:512 + P * (b + 1)])
                                fill_inc(last, name)
                        for t in range(TILES):
                            quantum("zA", c, t)
                    for q in range(EARLY):
                        quantum(*QUANTA[q])

                    pe.wait_ge(latents_ready, 1)
                    for t in range(TILES):
                        name = ("small", t)
                        fill_wait(pe, name)
                        pe.wait_ge(cq_scaled, t + 1)
                        for k in range(2):
                            flip(quad(name)[:, k, :], Z[:, t, P * k:P * (k + 1)])
                        flip(quad(name)[:, 2, :], Z[:, t, QLORA:QLORA + LORA])
                        fill_inc(flip(quad(name)[:, 3, :], Z[:, t, NZ + ROPE - P:NZ + ROPE]), name)

                    pe.wait_ge(wq_rot, 2)
                    pe.wait_ge(wq_in, 32)
                    for t in range(TILES):
                        copied_wait(pe, ("small", t))
                    for g in range(2):
                        name = f"qs{g}"
                        fill_wait(pe, name)
                        for j in range(4):
                            for k in range(2):
                                last = mm(quad(name)[:, j, :], WQ[:, k, 4 * g + j, :], CQT[:, k, SEQ:TOK],
                                          start=(k == 0), stop=(k == 1))
                        fill_inc(last, name)
                    copied_wait(pe, "uk0")
                    copied_wait(pe, "uk1")
                    for g in range(2):
                        name = f"ql{g}"
                        fill_wait(pe, name)
                        copied_wait(pe, f"qs{g}")
                        for j in range(4):
                            last = mm(quad(name)[:, j, :], UKT[0:NOPE, 4 * g + j, :], QS[0:NOPE, :, 4 * g + j, :],
                                      start=True, stop=True)
                        fill_inc(last, name)
                    def filler(n):
                        if n in FILL:
                            quantum(*QUANTA[FILL[n]])

                    def embed(half, t):
                        if t == 0:
                            j = CHUNKS.index((f"pe{half}", 0))
                            pe.wait_ge(w_loaded[j % RAW], 16 * (j // RAW + 1))
                        pe.wait_ge(acc_drained[t], BLK["pe0"] + half)
                        slot = CHUNKS.index((f"pe{half}", 0)) % RAW
                        for k in range(2):
                            last = mm(acc[t][:, :], PTR[:, k, P * t:P * (t + 1)], WR[:, slot, k, :],
                                      start=(k == 0), stop=(k == 1))
                        last.then_inc(acc_filled[t], 1)

                    def flip_cache(s):
                        name = ("c", s)
                        fill_wait(pe, name)
                        slot = s % CACHED
                        pe.wait_ge(cache_in[slot], 48 * (s // CACHED + 1))
                        for j in range(2):
                            flip(quad(name)[:, j, :], CKV[:, slot, j, :])
                            last = flip(quad(name)[:, 2 + j, :], CKR[:, slot, j, :])
                        fill_inc(last, name)

                    def flip_probs(n, w):
                        name = ("p", n)
                        fill_wait(pe, name)
                        for j in range(w // P):
                            last = flip(quad(name)[:, j, :], SB[:, n % 2, P * j:P * (j + 1)])
                        fill_inc(last, name)

                    def sample_values(s):
                        name = ("o", s)
                        fill_wait(pe, name)
                        copied_wait(pe, ("p", s))
                        out = bank(name)[:, 0:P]
                        for j in range(2):
                            mm(out, CKV[:, s % CACHED, j, :], PT[:, s % 2, j, :], start=(j == 0), stop=False)
                        fill_inc(mm(out, Z[:, TILES - 1, QLORA:QLORA + LORA], PT[:, s % 2, 2, :],
                                    start=False, stop=True), name)

                    def sample_scores(s):
                        name = ("s", s)
                        fill_wait(pe, name)
                        copied_wait(pe, ("c", s))
                        q_lat = QL[:, s, :, :].rearrange("p h t -> p (h t)")
                        q_rot = QS[NOPE:P, s, :, :].rearrange("p h t -> p (h t)")
                        mm(bank(name)[:, 0:PAST], q_lat, CTK[:, 0:PAST], start=True, stop=False)
                        mm(bank(name)[:, 0:PAST], q_rot, CTK[NOPE:P, PAST:2 * PAST], start=False, stop=True)
                        new = bank(name)[:, PAST:PAST + P]
                        mm(new, q_lat, CKVT[:, SEQ:TOK], start=True, stop=False)
                        mm(new, q_rot, KRS[NOPE:P, :], start=False, stop=False)
                        fill_inc(mm(new, ONES[:, :], MROW[:, 112 - NS * s:240 - NS * s], start=False, stop=True), name)

                    copied_wait(pe, "ql1")
                    flip_cache(0)
                    sample_scores(0)
                    flip_cache(1)
                    for s in range(NB):
                        if s < NB - 1:
                            sample_scores(s + 1)
                        if s:
                            sample_values(s - 1)
                        if s < NB - 2:
                            flip_cache(s + 2)
                        filler(s)
                        pe.wait_ge(p_scaled, s + 1)
                        flip_probs(s, PAST + P)

                    def keys(h):
                        name = ("k", h)
                        fill_wait(pe, name)
                        fill_inc(mm(bank(name)[0:NOPE, :], WKV[:, h, 0:NOPE], CKVT[:, 0:SEQ], start=True, stop=True), name)

                    def queries(h):
                        name = ("q", h)
                        fill_wait(pe, name)
                        for k in range(2):
                            last = mm(bank(name)[:, :], WQ[:, k, h, :], CQT[:, k, 0:SEQ], start=(k == 0), stop=(k == 1))
                        fill_inc(last, name)

                    def scores(u):
                        h, i = divmod(u, 4)
                        name = ("s", NB + u)
                        fill_wait(pe, name)
                        if i == 0:
                            copied_wait(pe, ("k", h))
                            copied_wait(pe, ("q", h))
                        w = P * (i + 1)
                        fill_inc(mm(bank(name)[:, 0:w], QH[:, h % 2, P * i:P * (i + 1)], KH[:, h % 2, 0:w],
                                    start=True, stop=True), name)

                    def values(u):
                        h, i = divmod(u, 4)
                        n = NB + u
                        name = ("oh", h)
                        if i == 0:
                            fill_wait(pe, name)
                        copied_wait(pe, ("p", n))
                        for j in range(i + 1):
                            last = mm(quad(name)[:, i, :], PT[:, n % 2, j, :], V[:, j, P * (h // 2):P * (h // 2 + 1)],
                                      start=(j == 0), stop=(j == i))
                        if i == 3:
                            fill_inc(last, name)

                    keys(0)
                    queries(0)
                    sample_values(NB - 1)
                    for j in range(4):
                        name = ("v", j)
                        fill_wait(pe, name)
                        fill_inc(mm(bank(name)[:, :], CKVT[:, P * j:P * (j + 1)], WKV[:, :, NOPE:P], start=True, stop=True), name)
                    fill_wait(pe, "oa")
                    copied_wait(pe, ("o", NB - 1))
                    for h in range(HEADS):
                        last = mm(bank("oa")[:, VH * h:VH * (h + 1)], OL[:, h, :], WKV[:, h, NOPE:P], start=True, stop=True)
                    fill_inc(last, "oa")
                    for j in range(4):
                        copied_wait(pe, ("v", j))
                    scores(0)
                    for u in range(UNITS):
                        h, i = divmod(u, 4)
                        if u < UNITS - 1:
                            scores(u + 1)
                        if u:
                            values(u - 1)
                        if i == 1 and h < HEADS - 1:
                            keys(h + 1)
                        if i == 2 and h < HEADS - 1:
                            queries(h + 1)
                        filler(NB + u)
                        if 0 <= u - EMBED < TILES:
                            if u == EMBED:
                                copied_wait(pe, "p2")
                            embed(0, u - EMBED)
                        t = NB + u - CONV_OUT
                        if 0 <= t < TILES:
                            name = ("cv", t)
                            fill_wait(pe, name)
                            pe.wait_ge(conv_done, 8 * TAPS)
                            for c in range(4):
                                last = flip(quad(name)[:, c, :], VTv[:, t, c, :])
                            fill_inc(last, name)
                        pe.wait_ge(exped, NB + u + 1)
                        flip_probs(NB + u, P * (i + 1))
                    values(UNITS - 1)

                    for t in range(TILES):
                        embed(1, t)
                    for g in range(2):
                        for t in range(TILES):
                            pe.wait_ge((ya_scaled, yc_scaled)[g], t + 1)
                            flip_half(("y", t, g), Y[:, t, :])
                        for c in (2 * g, 2 * g + 1):
                            for t in range(TILES):
                                copied_wait(pe, ("y", t, g))
                                quantum("o0", c, t)

                    def flip_h(t):
                        pe.wait_ge(acc_drained[t], BLK["o1"] + 1)
                        for g in range(2):
                            flip_half(("h", t, g), H[:, t, :])

                    for c in range(4):
                        for t in range(TILES):
                            quantum("o1", c, t)
                            if c == 3 and t >= 3:
                                flip_h(t - 3)
                    for t in range(TILES - 3, TILES):
                        flip_h(t)
                    for name in ("pg0", "pg1"):
                        for c in range(4):
                            for t in range(TILES):
                                if name == "pg0":
                                    copied_wait(pe, ("h", t, c // 2))
                                quantum(name, c, t)

                @block.scalar
                def _(act):
                    av = nc.scalar.activation
                    th = [0]
                    n_sq = [0]

                    def mean_square(src, col, n, scale=1.0):
                        if n_sq[0]:
                            act.wait_ge(squares, n_sq[0])
                        n_sq[0] += 1
                        av(JUNK[:, 0:n], src, ACT.Square, scale=scale * n ** -0.5,
                           accum_out=MS[:, col:col + 1]).then_inc(squares, 1)

                    def copy(out, in_, scale=None):
                        return av(out, in_, ACT.Copy) if scale is None else av(out, in_, ACT.Copy, scale=scale)

                    def quad(name):
                        return bank(name)[:, :].rearrange("p (j t) -> p j t", t=P)

                    def high(i):
                        j, raw = raw_slot(i)
                        act.wait_ge(w_loaded[j % RAW], 16 * (j // RAW + 1))
                        if i >= SPLIT:
                            part_used(act, i - SPLIT)
                        for k in range(2):
                            last = copy(WHI[:, i % SPLIT, k, 0:width(PARTS[i][0])], raw[:, k, :], gain_column(i, k))
                        last.then_inc(hi_ready, 1)

                    def high_half(name):
                        _, t, g = name
                        filled_wait(act, name)
                        copy(XHI[:, t, 4 * g:4 * g + 4, :], quad(name)).then_inc(half_hi, 1)

                    copied_wait(act, "gain")
                    for t in range(TILES):
                        for g in range(2):
                            high_half(("x", t, g))
                        if t < 2:
                            high(t)
                    for t in range(TILES):
                        mean_square(H[:, t, :], t, D)
                    high(2)
                    for g in range(2):
                        name = f"uk{g}"
                        filled_wait(act, name)
                        drain_inc(copy(UKT[0:NOPE, 4 * g:4 * g + 4, :], quad(name)[0:NOPE, :, :]), name)
                    for g in range(2):
                        name = f"st{g}"
                        filled_wait(act, name)
                        for c in range(4):
                            last = copy(UTS[:, c, 4 * g:4 * g + 4, 0:STATE],
                                        bank(name)[:, 120 * c:120 * (c + 1)].rearrange("p (b j) -> p b j", b=4))
                        drain_inc(last, name)
                    high(3)
                    for g in range(3):
                        name = f"p{g}"
                        filled_wait(act, name)
                        m = min(2, TILES - 2 * g)
                        for k in range(2):
                            src = bank(name)[:, 0:2 * P * m].rearrange("p (t k e) -> p k t e", k=2, e=P)[:, k]
                            last = copy(PTR[:, k, 2 * P * g:2 * P * g + P * m].rearrange("p (t e) -> p t e", e=P), src)
                        drain_inc(last, name)

                    act.wait_ge(wq_in, 32)
                    copy(WQ[:, :, :, 96:112], WQ[:, :, :, 80:96]).then_inc(wq_rot, 1)
                    copy(WQ[:, :, :, 112:128], WQ[:, :, :, 64:80]).then_inc(wq_rot, 1)

                    def tanh_acc(t, block_no, hr):
                        k = th[0]
                        th[0] += 1
                        if k >= 2:
                            act.wait_ge(gated, k - 1)
                        av(TH[:, k % 2, :], acc[t][:, :], ACT.Tanh, scale=hr).then_inc(acc_drained[t], 1)

                    def leave(part, copy_out):
                        high(part)
                        for t in range(TILES):
                            copy_out(t)
                            if t == 1:
                                high(part + 1)

                    def value_out(t):
                        act.wait_ge(acc_filled[t], BLK["uv"] + 1)
                        copy(Y[:, t, 512:1024], acc[t][:, :], HR[:, t:t + 1]).then_inc(acc_drained[t], 1)

                    def gate_out(t):
                        act.wait_ge(acc_filled[t], BLK["ug"] + 1)
                        tanh_acc(t, BLK["ug"], HR[:, t:t + 1])

                    def latent_out(t):
                        act.wait_ge(acc_filled[t], BLK["zA"] + 1)
                        copy(Z[:, t, 0:NZ], acc[t][:, 0:NZ], RS[:, t:t + 1]).then_inc(acc_drained[t], 1)

                    act.wait_ge(rstd_ready, 1)
                    act.wait_ge(spilled, 16)
                    leave(4, value_out)
                    high(6)
                    high(7)
                    leave(8, gate_out)
                    high(10)
                    high(11)
                    for t in range(TILES):
                        name = ("u", t)
                        filled_wait(act, name)
                        if t < TILES - 1:
                            drain_inc(copy(UT[:, :, STATE + P * t:STATE + P * (t + 1)], quad(name)), name)
                        else:
                            for c in range(4):
                                last = copy(UTS[:, c, :, STATE:STATE + NS],
                                            quad(name)[:, c, :].rearrange("p (b j) -> p b j", b=NB))
                            drain_inc(last, name)

                    leave(12, latent_out)
                    for t in range(TILES):
                        act.wait_ge(acc_drained[t], BLK["zA"] + 1)
                        mean_square(Z[:, t, 0:QLORA], 5 + t, QLORA)
                        mean_square(Z[:, t, QLORA:QLORA + LORA], 10 + t, LORA)
                    high(14)
                    act.wait_ge(rstd_ready, 2)
                    for t in range(TILES):
                        copy(Z[:, t, 0:QLORA], Z[:, t, 0:QLORA], RS[:, 5 + t:6 + t]).then_inc(cq_scaled, 1)
                    for t in range(TILES):
                        name = ("small", t)
                        filled_wait(act, name)
                        cols = slice(P * t, P * (t + 1))
                        for k in range(2):
                            copy(CQT[:, k, cols], quad(name)[:, k, :], GT[:, G_Q + k:G_Q + k + 1])
                        copy(CKVT[:, cols], quad(name)[:, 2, :])
                        if t < TILES - 1:
                            copy(KH[NOPE:P, 0, cols], quad(name)[NOPE:P, 3, :])
                            drain_inc(copy(KH[NOPE:P, 1, cols], quad(name)[NOPE:P, 3, :]), name)
                        else:
                            drain_inc(copy(KRS[NOPE:P, :], quad(name)[NOPE:P, 3, :]), name)

                    for g in range(2):
                        name = f"ql{g}"
                        filled_wait(act, name)
                        for j in range(4):
                            last = copy(QL[:, :, 4 * g + j, :], quad(name)[:, j, :].rearrange("p (s t) -> p s t", t=NS))
                        drain_inc(last, name)
                    high(15)

                    def filler_out(n):
                        if n % 5 == 0 and 5 <= n <= 25:
                            high(15 + n // 5)
                        if n not in FILL:
                            return
                        name, c, t = QUANTA[FILL[n]]
                        if c < 3:
                            return
                        act.wait_ge(acc_filled[t], BLK[name] + 1)
                        if name == "gc" and t == 0:
                            act.wait_ge(u_stored, 16 * (1 + NB))
                        col = 0 if name == "ga" else 512
                        copy(Y[:, t, col:col + 512], acc[t][:, :], HR[:, t:t + 1])
                        tanh_acc(t, BLK[name], HR[:, t:t + 1])

                    def probs(n, w):
                        copied_wait(act, ("s", n))
                        av(SB[:, n % 2, 0:w], SB[:, n % 2, 0:w], ACT.Exp, scale=-1.0, bias=NBIAS[:, n:n + 1],
                           accum_out=SUMS[:, n:n + 1]).then_inc(exped, 1)

                    def probs_out(n, k):
                        name = ("p", n)
                        filled_wait(act, name)
                        drain_inc(copy(PT[:, n % 2, 0:k, :], quad(name)[:, 0:k, :]), name)

                    def cache_out(s):
                        name = ("c", s)
                        filled_wait(act, name)
                        drain_inc(copy(CTK[:, :], bank(name)[:, :]), name)

                    def sample_out(s):
                        name = ("o", s)
                        filled_wait(act, name)
                        drain_inc(copy(OL[:, :, NS * s:NS * (s + 1)],
                                       bank(name)[:, 0:P].rearrange("p (h t) -> p h t", h=HEADS)), name)

                    def keys_out(h):
                        name = ("k", h)
                        filled_wait(act, name)
                        drain_inc(copy(KH[0:NOPE, h % 2, :], bank(name)[0:NOPE, :]), name)

                    cache_out(0)
                    cache_out(1)
                    for s in range(NB):
                        probs(s, PAST + P)
                        if s:
                            sample_out(s - 1)
                        if s < NB - 2:
                            cache_out(s + 2)
                        filler_out(s)
                        probs_out(s, 3)

                    def embedding_out(half, t):
                        act.wait_ge(acc_filled[t], BLK["pe0"] + half + 1)
                        copy(EMB[half][t], acc[t][:, :]).then_inc(acc_drained[t], 1)

                    def v_tanh_out(t):
                        k = th[0]
                        th[0] += 1
                        act.wait_ge(gated, k - 1)
                        act.wait_ge(ln_done, t + 1)
                        av(TH[:, k % 2, :], VT[:, 512 * t:512 * (t + 1)], ACT.Tanh, scale=0.5).then_inc(v_tanh, 1)

                    keys_out(0)
                    sample_out(NB - 1)
                    for j in range(4):
                        name = ("v", j)
                        filled_wait(act, name)
                        drain_inc(copy(V[:, j, :], bank(name)[:, :]), name)
                    filled_wait(act, "oa")
                    drain_inc(copy(OTOK[:, TILES - 1, :], bank("oa")[:, :]), "oa")
                    for u in range(UNITS):
                        h, i = divmod(u, 4)
                        if i == 1 and h < HEADS - 1:
                            keys_out(h + 1)
                        probs(NB + u, P * (i + 1))
                        filler_out(NB + u)
                        t = NB + u - CONV_OUT
                        if 0 <= t < TILES:
                            name = ("cv", t)
                            filled_wait(act, name)
                            drain_inc(copy(VTv[:, t, :, :], quad(name)), name)
                        if 0 <= u - EMBED < TILES:
                            if u == EMBED:
                                act.wait_ge(conv_done, 8 * TAPS)
                            embedding_out(0, u - EMBED)
                        probs_out(NB + u, i + 1)
                        if u >= UNITS - V_EARLY:
                            v_tanh_out(u - (UNITS - V_EARLY))

                    for t in range(TILES):
                        act.wait_ge(ya_ready, t + 1)
                        mean_square(Y[:, t, 0:512], 15 + t, 512)
                    for t in range(TILES):
                        embedding_out(1, t)
                    high(21)
                    for t in range(TILES):
                        high_half(("y", t, 0))
                    for t in range(TILES):
                        if t == V_EARLY + 1:
                            high(22)
                        if t >= V_EARLY:
                            v_tanh_out(t)
                        else:
                            act.wait_ge(yc_ready, t + 1)
                        if t > V_EARLY:
                            act.wait_ge(yc_ready, t)
                        if t:
                            mean_square(Y[:, t - 1, 512:1024], 20 + t - 1, 512)
                    act.wait_ge(yc_ready, TILES)
                    mean_square(Y[:, TILES - 1, 512:1024], 20 + TILES - 1, 512)
                    high(23)
                    act.wait_ge(rstd_ready, 5)
                    for t in range(TILES):
                        copy(Y[:, t, 512:1024], Y[:, t, 512:1024], RS[:, 20 + t:21 + t]).then_inc(yc_scaled, 1)
                    for t in range(TILES):
                        high_half(("y", t, 1))
                    high(24)
                    high(25)
                    for i in range(26, 29):
                        high(i)
                    for t in range(TILES):
                        for g in range(2):
                            high_half(("h", t, g))
                        if t == 2:
                            high(29)
                    for t in range(TILES):
                        act.wait_ge(acc_drained[t], BLK["o1"] + 1)
                        mean_square(H[:, t, :], 25 + t, D)
                    high(30)
                    high(31)
                    act.wait_ge(rstd_ready, 6)

                    def pg_out(half, t):
                        act.wait_ge(acc_filled[t], BLK["pg0"] + half + 1)
                        tanh_acc(t, BLK["pg0"] + half, HR[:, t:t + 1])

                    leave(32, lambda t: pg_out(0, t))
                    high(34)
                    high(35)
                    for t in range(TILES):
                        pg_out(1, t)

                @block.vector
                def _(dve):
                    chain = Chain(dve, dve_chain)
                    tt, stt = nc.vector.tensor_tensor, nc.vector.scalar_tensor_tensor

                    def quad(name):
                        return bank(name)[:, :].rearrange("p (j t) -> p j t", t=P)

                    filled_wait(dve, "gain")
                    drain_inc(nc.vector.tensor_copy(GT[:, :], bank("gain")[:, 0:30]), "gain")
                    filled_wait(dve, "taps")
                    drain_inc(nc.vector.tensor_copy(CWT[:, :, :], bank("taps")[:, 0:4 * TAPS].rearrange("p (c k) -> p c k", c=4)), "taps")
                    copied_wait(dve, "gain")

                    def low(i):
                        _, raw = raw_slot(i)
                        dve.wait_ge(hi_ready, i + 1)
                        for k in range(2):
                            at_k = (slice(None), i % SPLIT, k, slice(0, width(PARTS[i][0])))
                            last = stt(out=WLO[at_k], in0=raw[:, k, :], scalar=gain_column(i, k),
                                       in1=WHI[at_k].bitcast(F32), op0=ALU.mult, op1=ALU.subtract)
                        last.then_inc(split_ready, 1)

                    halves = [0]

                    def low_half(name):
                        _, t, g = name
                        halves[0] += 1
                        dve.wait_ge(half_hi, halves[0])
                        drain_inc(tt(XLO[:, t, 4 * g:4 * g + 4, :], quad(name), XHI[:, t, 4 * g:4 * g + 4, :].bitcast(F32),
                                     ALU.subtract), name)

                    for t in range(TILES):
                        for g in range(2):
                            low_half(("x", t, g))
                        if t < 2:
                            low(t)
                    dve.wait_ge(squares, 5)
                    chain.link(rsqrt(dve, chain, MS[:, 0:5], RS[:, 0:5], 5))
                    nc.vector.tensor_scalar(HR[:, 0:5], RS[:, 0:5], 0.5, None, ALU.mult).then_inc(rstd_ready, 1)
                    for i in range(2, 9):
                        low(i)

                    k_th = [0]

                    def gate(out, other, ready, value):
                        k = k_th[0]
                        k_th[0] += 1
                        dve.wait_ge(ready, value)
                        return stt(out=out, in0=TH[:, k % 2, :], scalar=1.0, in1=other, op0=ALU.add, op1=ALU.mult)

                    for t in range(TILES):
                        u = Y[:, t, 512:1024]
                        gate(u, u, acc_drained[t], BLK["ug"] + 1).then_inc(gated, 1)
                        if t == 1:
                            low(9)
                    def tap(k):
                        n = 8 * k
                        for c in range(4):
                            w = CWT[:, c, k:k + 1]
                            bias = GT[:, G_CB + c:G_CB + c + 1]
                            for part in range(2):
                                if part == 0:
                                    out = VTv[:, 0:4, c, :]
                                    src = UT[:, c, k:k + SEQ].rearrange("p (t e) -> p t e", e=P)
                                else:
                                    out = VTv[:, 4, c, :].rearrange("p (b j) -> p b j", b=NB)
                                    src = UTS[:, c, :, k:k + NS]
                                if k == 0:
                                    ins = nc.vector.tensor_scalar(out, src, w, bias, ALU.mult, ALU.add)
                                else:
                                    dve.wait_ge(conv_done, n - 7)
                                    ins = stt(out=out, in0=src, scalar=w, in1=out, op0=ALU.mult, op1=ALU.add)
                                ins.then_inc(conv_done, 1)
                                n += 1

                    low(10)
                    low(11)
                    for t in range(TILES):
                        copied_wait(dve, ("u", t))
                    for k in TAP["early"]:
                        tap(k)
                        if k == 1:
                            low(12)
                        if k == 2:
                            low(13)

                    dve.wait_ge(squares, 15)
                    rsqrt(dve, chain, MS[:, 5:15], RS[:, 5:15], 10).then_inc(rstd_ready, 1)
                    dve.wait_ge(rstd_ready, 2)
                    dve.wait_ge(lnkv_in, 16)
                    for t in range(TILES):
                        lat = Z[:, t, QLORA:QLORA + LORA]
                        stt(out=lat, in0=lat, scalar=RS[:, 10 + t:11 + t], in1=LNKV[:, :], op0=ALU.mult, op1=ALU.mult)
                    kr = Z[:, :, NZ - ROPE:NZ].rearrange("p t (a e) -> p t a e", a=2)
                    tt(KRA[:, :, :, :], kr, ROPEK[:, :, 0:2, :], ALU.mult)
                    tt(KRB[:, :, 0, :], kr[:, :, 1, :], ROPEK[:, :, 2, :], ALU.mult)
                    chain.link(tt(KRB[:, :, 1, :], kr[:, :, 0, :], ROPEK[:, :, 3, :], ALU.mult))
                    kr2 = Z[:, :, NZ:NZ + ROPE].rearrange("p t (a e) -> p t a e", a=2)
                    tt(kr2, KRA[:, :, :, :], KRB[:, :, :, :], ALU.add)
                    tt(kr, KRA[:, :, :, :], KRB[:, :, :, :], ALU.add).then_inc(latents_ready, 1)

                    low(14)
                    for k in TAP["latents"]:
                        tap(k)
                    for g in range(2):
                        name = f"qs{g}"
                        filled_wait(dve, name)
                        rope = ROPET[:, SEQ:TOK].rearrange("p (s t) -> p s t", t=NS)
                        for j in range(4):
                            last = tt(QS[:, :, 4 * g + j, :], quad(name)[:, j, :].rearrange("p (s t) -> p s t", t=NS),
                                      rope, ALU.mult)
                        drain_inc(last, name)

                    low(15)
                    for k in TAP["queries"]:
                        tap(k)

                    def mask(n, w, add):
                        name = ("s", n)
                        filled_wait(dve, name)
                        drain_inc(nc.vector.tensor_tensor_reduce(SB[:, n % 2, 0:w], bank(name)[:, 0:w], add, -SCALE, 3e38,
                                                                 ALU.add, ALU.min, NBIAS[:, n:n + 1]), name)

                    def filler_gate(n):
                        if n % 5 == 0 and 5 <= n <= 25:
                            low(15 + n // 5)
                        if n not in FILL:
                            return
                        name, c, t = QUANTA[FILL[n]]
                        if c == 3:
                            col = 0 if name == "ga" else 512
                            y = Y[:, t, col:col + 512]
                            gate(y, y, acc_drained[t], BLK[name] + 1).then_inc(gated, 1)

                    mask(0, PAST + P, MASK[:, 0:PAST + P])
                    for s in range(NB):
                        dve.wait_ge(exped, s + 1)
                        chain.link(nc.vector.reciprocal(RSUM[:, s:s + 1], SUMS[:, s:s + 1]))
                        nc.vector.tensor_scalar(SB[:, s % 2, 0:PAST + P], SB[:, s % 2, 0:PAST + P],
                                                RSUM[:, s:s + 1], None, ALU.mult).then_inc(p_scaled, 1)
                        if s < NB - 1:
                            mask(s + 1, PAST + P, MASK[:, 0:PAST + P])
                        for k in TAP[s]:
                            tap(k)
                        filler_gate(s)

                    def queries_out(h):
                        name = ("q", h)
                        filled_wait(dve, name)
                        drain_inc(tt(QH[:, h % 2, :], bank(name)[:, :], ROPET[:, 0:SEQ], ALU.mult), name)

                    def head_out(h):
                        name = ("oh", h)
                        n = NB + 4 * h
                        dve.wait_ge(exped, n + 4)
                        chain.link(nc.vector.reciprocal(RSUM[:, n:n + 4], SUMS[:, n:n + 4]))
                        filled_wait(dve, name)
                        own = quad(name)[:, :, VH * (h % 2):VH * (h % 2 + 1)]
                        drain_inc(tt(OTOK[:, 0:4, VH * h:VH * (h + 1)], own,
                                     RSUM[:, n:n + 4].unsqueeze(2).to_broadcast([P, 4, VH]), ALU.mult), name)

                    def normed(t):
                        v = VT[:, 512 * t:512 * (t + 1)]
                        chain.link(nc.vector.tensor_scalar(v, v, MV[:, t, 0:1], RSV[:, t:t + 1], ALU.subtract, ALU.mult))
                        tt(v, v, LCG, ALU.mult).then_inc(ln_scaled, 1)

                    def layer_norm(n):
                        n -= CONV_OUT
                        if 0 <= n < TILES:
                            copied_wait(dve, ("cv", n))
                            nc.vector.bn_stats(BN6[:, n, :], VT[:, 512 * n:512 * (n + 1)]).then_inc(stats_ready, 1)
                        elif n == TILES:
                            dve.wait_ge(stats_ready, TILES)
                            for t in range(TILES):
                                last = nc.vector.bn_aggr(MV[:, t, :], BN6[:, t, :])
                            chain.link(last)
                            rsqrt(dve, chain, MV[:, :, 1], RSV[:, :], TILES).then_inc(rstd_ready, 1)
                        elif n == TILES + 1:
                            dve.wait_ge(rstd_ready, 3)
                            dve.wait_ge(lnconv_in, 32)
                            for t in range(2):
                                normed(t)
                        elif n > TILES + 1:
                            normed(n - TILES)

                    queries_out(0)
                    for k in TAP["turn"]:
                        tap(k)
                    mask(NB, P, MASK[:, 512 - P:512])
                    for u in range(UNITS):
                        h, i = divmod(u, 4)
                        if u < UNITS - 1:
                            w = P * ((i + 1) % 4 + 1)
                            mask(NB + u + 1, w, MASK[:, 512 - w:512])
                        if i == 0 and h:
                            head_out(h - 1)
                        if i == 2 and h < HEADS - 1:
                            queries_out(h + 1)
                        for k in TAP[NB + u]:
                            tap(k)
                        filler_gate(NB + u)
                        layer_norm(NB + u)
                    head_out(HEADS - 1)
                    copied_wait(dve, ("oh", HEADS - 1))
                    copied_wait(dve, "oa")
                    dve.wait_ge(gated, 15)
                    for t in range(TILES):
                        y = Y[:, t, 0:512]
                        tt(y, y, OTOK[:, t, :], ALU.mult).then_inc(ya_ready, 1)

                    normed(NORMED)
                    dve.wait_ge(squares, 20)
                    rsqrt(dve, chain, MS[:, 15:20], RS[:, 15:20], TILES).then_inc(rstd_ready, 1)
                    dve.wait_ge(rstd_ready, 4)
                    for t in range(TILES):
                        y = Y[:, t, 0:512]
                        nc.vector.tensor_scalar(y, y, RS[:, 15 + t:16 + t], None, ALU.mult).then_inc(ya_scaled, 1)
                    low(21)
                    for t in range(NORMED + 1, TILES):
                        normed(t)
                    for t in range(TILES):
                        low_half(("y", t, 0))

                    def conv_gate(t):
                        v = VT[:, 512 * t:512 * (t + 1)]
                        gate(v, v, v_tanh, t + 1).then_inc(gated, 1)
                        dve.wait_ge(gated, 16 + t)
                        y = Y[:, t, 512:1024]
                        stt(out=y, in0=v, scalar=0.5, in1=y, op0=ALU.mult, op1=ALU.mult).then_inc(yc_ready, 1)

                    for t in range(TILES):
                        if t == V_EARLY + 1:
                            low(22)
                        conv_gate(t)
                    dve.wait_ge(squares, 25)
                    rsqrt(dve, chain, MS[:, 20:25], RS[:, 20:25], TILES).then_inc(rstd_ready, 1)
                    low(23)
                    for t in range(TILES):
                        low_half(("y", t, 1))
                    low(24)

                    def onto_residual(half, t):
                        dve.wait_ge(acc_filled[t], BLK["o0"] + half + 1)
                        hh = H[:, t, 512 * half:512 * (half + 1)]
                        tt(hh, hh, acc[t][:, :], ALU.add).then_inc(acc_drained[t], 1)

                    dve.wait_ge(h_in[0], 16 * TILES)
                    for t in range(TILES):
                        onto_residual(0, t)
                        if t == 1:
                            low(25)
                    for i in range(26, 29):
                        low(i)
                    dve.wait_ge(h_in[1], 16 * TILES)
                    for t in range(TILES):
                        onto_residual(1, t)
                        if t > 2:
                            for g in range(2):
                                low_half(("h", t - 3, g))
                    for t in range(TILES - 3, TILES):
                        for g in range(2):
                            low_half(("h", t, g))
                        if t == 2:
                            low(29)
                    dve.wait_ge(squares, 30)
                    chain.link(rsqrt(dve, chain, MS[:, 25:30], RS[:, 25:30], 5))
                    nc.vector.tensor_scalar(HR[:, 0:5], RS[:, 25:30], 0.5, None, ALU.mult).then_inc(rstd_ready, 1)
                    for i in range(30, 33):
                        low(i)
                    for half in range(2):
                        for t in range(TILES):
                            emb = EMB[half][t]
                            gate(emb, emb, acc_drained[t], BLK["pg0"] + half + 1).then_inc(gated, 1)
                            if half == 0 and t == 1:
                                low(33)
                            dve.wait_ge(gated, 21 + 5 * half + t)
                            hh = H[:, t, 512 * half:512 * (half + 1)]
                            stt(out=hh, in0=emb, scalar=0.5, in1=hh, op0=ALU.mult, op1=ALU.add).then_inc(h_done, 1)
                        if half == 0:
                            low(34)
                            low(35)

                @block.gpsimd
                def _(pool):
                    def load_cache(s):
                        src = a["cache_ckv"][bass.ds(layer, 1), s]
                        slot = s % CACHED
                        pool.dma_start(CKV[:, slot, :, :], src.rearrange("o (j p) r -> p (o j) r", p=P)).then_inc(cache_in[slot], 16)
                        src = a["cache_krope"][bass.ds(layer, 1), s].rearrange("o (j p) r -> p (o j) r", p=P)
                        for k in range(2):
                            lo = NOPE + ROPE * k
                            pool.dma_start(CKR[:, slot, :, lo:lo + ROPE], src).then_inc(cache_in[slot], 16)

                    for s in range(CACHED):
                        load_cache(s)
                    pool.dma_start(a["new_conv_sample"][bass.ds(layer, 1), :, 0:STATE - NS, :],
                                   a["state_conv"][bass.ds(layer, 1), :, NS:STATE, :]).then_inc(states_stored, 16)
                    pool.wait_ge(latents_ready, 1)
                    for name, rows, col, n in (("new_ckv", None, QLORA, LORA), ("new_krope", None, NZ - ROPE, ROPE)):
                        pool.dma_start(at(name + "_prompt").rearrange("l o (t p) r -> p (l o t) r", p=P),
                                       Z[:, 0:4, col:col + n]).then_inc(latents_stored, 16)
                        pool.dma_start(at(name + "_sample").rearrange("o b s r -> (o b s) r"),
                                       Z[:, 4, col:col + n]).then_inc(latents_stored, 16)
                    pool.wait_ge(gated, TILES)
                    pool.dma_start(at("new_conv_prompt").rearrange("l o s c -> (l o s) c"),
                                   Y[P - STATE:P, TILES - 2, 512:1024]).then_inc(u_stored, 16)
                    for s in range(NB):
                        pool.dma_start(a["new_conv_sample"][bass.ds(layer, 1), s, STATE - NS:STATE, :].rearrange("o s c -> (o s) c"),
                                       Y[NS * s:NS * (s + 1), TILES - 1, 512:1024]).then_inc(u_stored, 16)
                    for s in range(CACHED, NB):
                        filled_wait(pool, ("o", s - CACHED))
                        load_cache(s)
                    filled_wait(pool, ("o", NB - 1))
                    pool.dma_start(LCG, at("ln_conv_g").to_broadcast([P, CH])).then_inc(lnconv_in, 16)
                    pool.dma_start(LCB, at("ln_conv_b").to_broadcast([P, CH])).then_inc(lnconv_in, 16)
                    pool.wait_ge(lnconv_in, 32)
                    for t in range(TILES):
                        pool.wait_ge(ln_scaled, t + 1)
                        v = VT[:, 512 * t:512 * (t + 1)]
                        nc.gpsimd.tensor_tensor(v, v, LCB, ALU.add).then_inc(ln_done, 1)
                    pool.wait_ge(latents_stored, 64)
                    pool.wait_ge(u_stored, 16 * (1 + NB))
                    pool.wait_ge(states_stored, 16)

            nc.gpsimd.dma_reset(range(sems[0].num, sems[-1].num + 1))
            nc.gpsimd.sem_clear(range(sems[0].num, sems[-1].num + 1))
            nc.all_engine_barrier()

        LNF = WR[:, 0, :, :].rearrange("p k n -> p (k n)")
        with nc.Block() as block:
            @block.sync
            def _(sp):
                sp.dma_start(LNF, a["ln_f"].unsqueeze(0).to_broadcast([P, D])).then_inc(const_in, 16)
                for t in range(TILES):
                    sp.wait_ge(h_done, t + 1)
                    dst = a["y_prompt"][0, P * t:P * (t + 1), :] if t < 4 else a["y_sample"].rearrange("b s d -> (b s) d")
                    sp.dma_start(dst, H[:, t, :]).then_inc(y_stored, 16)
                sp.wait_ge(y_stored, 16 * TILES)

            @block.scalar
            def _(act):
                for t in range(TILES):
                    if t:
                        act.wait_ge(squares, t)
                    nc.scalar.activation(JUNK[:, :], H[:, t, :], ACT.Square, scale=D ** -0.5,
                                         accum_out=MS[:, t:t + 1]).then_inc(squares, 1)

            @block.vector
            def _(dve):
                chain = Chain(dve, dve_chain)
                dve.wait_ge(squares, TILES)
                chain.link(rsqrt(dve, chain, MS[:, 0:5], RS[:, 0:5], 5))
                dve.wait_ge(const_in, 16)
                for t in range(TILES):
                    nc.vector.scalar_tensor_tensor(out=H[:, t, :], in0=H[:, t, :], scalar=RS[:, t:t + 1], in1=LNF,
                                                   op0=ALU.mult, op1=ALU.mult).then_inc(h_done, 1)


_INS = ["x_prompt", "x_sample", "cache_ckv", "cache_krope", "state_conv", "p_prompt", "p_sample", "ln_in", "w_in",
        "ln_q", "w_q_b", "ln_kv", "w_kv_b", "conv_w", "conv_b", "ln_conv_g", "ln_conv_b", "ln_out_a", "ln_out_c",
        "w_out", "w_pe", "ln_pg", "w_pg", "ln_f"]
_OUTS = [("y_prompt", (1, SEQ, D)), ("y_sample", (NB, NS, D)),
         ("new_ckv_prompt", (DEPTH, 1, SEQ, LORA)), ("new_krope_prompt", (DEPTH, 1, SEQ, ROPE)),
         ("new_conv_prompt", (DEPTH, 1, STATE, CH)),
         ("new_ckv_sample", (DEPTH, NB, NS, LORA)), ("new_krope_sample", (DEPTH, NB, NS, ROPE)),
         ("new_conv_sample", (DEPTH, NB, STATE, CH))]


def constants():
    import numpy as np
    f = np.float32
    half = ROPE // 2
    inv = (f(10000.0) ** (-np.arange(half, dtype=f) / f(half))).astype(f)
    pos = np.concatenate([np.arange(SEQ), np.tile(PAST + np.arange(NS), NB)]).astype(f)
    ang = pos[:, None] * inv[None, :]
    cos, sin = np.cos(ang).astype(f), np.sin(ang).astype(f)
    ropet = np.ones((P, TOK), f)
    ropet[64:80] = cos.T
    ropet[80:96] = cos.T
    ropet[96:112] = -sin.T
    ropet[112:128] = sin.T
    ropek = np.stack([cos, cos, -sin, sin], axis=1).reshape(TILES, P, 4, half).transpose(1, 0, 2, 3)
    mrow = np.full((1, 240), NEG, f)
    mrow[0, 112:128] = 0.0
    return {"c_ident": np.eye(P, dtype=f), "c_ropet": ropet, "c_ropek": np.ascontiguousarray(ropek), "c_mrow": mrow}


def kernel(**inputs):
    import numpy as _np
    import concourse.bacc as _bacc
    from concourse import mybir as _mybir
    from concourse.bass_utils import run_bass_kernel_spmd as _run

    nc = _bacc.Bacc("TRN2", target_bir_lowering=False, num_devices=1)
    given = {name: _np.ascontiguousarray(inputs[name]) for name in _INS}
    given.update(constants())
    arrays, aps = {}, {}
    for name, x in given.items():
        arrays[f"in_{name}_dram"] = x
        aps[name] = nc.dram_tensor(f"in_{name}_dram", x.shape, _mybir.dt.from_np(x.dtype), kind="ExternalInput").ap()
    for name, shape in _OUTS:
        aps[name] = nc.dram_tensor(f"out_{name}_dram", shape, F32, kind="ExternalOutput").ap()
    build(nc, aps)
    r = _run(nc, [arrays], core_ids=[0])
    return tuple(r.results[0][f"out_{name}_dram"] for name, _ in _OUTS)
```

```python
from contextlib import ExitStack

import concourse.bass as bass
from concourse import mybir

ALU = mybir.AluOpType
ACT = mybir.ActivationFunctionType
F32 = mybir.dt.float32
F32R = mybir.dt.float32r
I32 = mybir.dt.int32
BF16 = mybir.dt.bfloat16

P = 128
D = 1024
SEQ = 512
DEPTH = 2
NB, NS, PAST = 8, 16, 256
PLE = 256
HEADS, NOPE, ROPE, VH = 8, 64, 32, 64
LORA, QLORA = 128, 256
CH, TAPS = 512, 31
STATE = TAPS - 1
SCALE = float(NOPE + ROPE) ** -0.5
EPS = 1e-6
NEG = -1e30
TILES = SEQ // P + 1
TOK = TILES * P
KT = D // P
RAW = 3
SPLIT = 2
CACHED = 4
NZ = QLORA + LORA + ROPE
MAGIC = float(0x5F3759DF)

BLOCKS = ["u0", "u1", "zA", "gc", "ga", "pe0", "pe1", "o0", "o1", "pg0", "pg1"]
BLK = {name: i for i, name in enumerate(BLOCKS)}
ZCOL = {"zA": (0, NZ), "ga": (NZ, 512), "u0": (NZ + 512, 512), "u1": (NZ + 768, 512), "gc": (NZ + 1536, 512)}


CHUNKS = [(b, c) for b in BLOCKS for c in ((0,) if b[:2] == "pe" else range(4))]
PARTS = [c for c in CHUNKS if c[0][:2] != "pe"]
PART = {c: i for i, c in enumerate(PARTS)}
UNITS = HEADS * (SEQ // P)
QUANTA = [(b, c, t) for b in ("gc", "ga") for c in range(4) for t in range(TILES)]
EARLY = 2 * TILES
_steps = list(range(NB)) + [NB + u for u in range(UNITS) if u % 4 != 3]
FILL = dict(zip(_steps, range(EARLY, len(QUANTA))))
NEXT_PART = {n: PART[("gc", 0)] + q // TILES + 1 for n, q in FILL.items() if q % TILES == 0 and q > EARLY}
_left = [list(range(TAPS)), list(range(TAPS))]


def _take(n, half=None):
    out = []
    for _ in range(n):
        h = half if half is not None else int(len(_left[1]) >= len(_left[0]))
        if _left[h]:
            out.append((_left[h].pop(0), h))
    return out


TAP = {place: _take(n, 0) for place, n in zip(("u1a", "u1b", "z0", "z1", "z2"), (3, 2, 2, 3, 2))}
for _place, _n in zip(("z3", "z4", "z5", "latents", "queries"), (2,2,2,4,2)):
    TAP[_place] = _take(_n)
for _n in range(NB):
    TAP[_n] = _take(1+_n%2)
TAP["turn"] = _take(4)
for _u in range(UNITS):
    TAP[NB + _u] = _take(1)
EMBED = UNITS - 5
V_EARLY = 2
CONV_OUT = NB + 22


def shared_bank_plan():
    order = {"S": [], "T": [], "O": []}
    turn = [0]

    def cyc(*names):
        for n in names:
            order["STO"[turn[0] % 3]].append(n)
            turn[0] += 1

    cyc("gain")
    for t in range(TILES):
        for g in range(2):
            cyc(("x", t, g))
    cyc("taps", "uk0", "uk1", "st0", "st1", "p0", "p1", "p2")
    for half in range(2):
        for t in range(TILES):
            cyc(("u", half, t))
    for t in range(TILES):
        cyc(("small", t))
    cyc("qs0", "qs1", "ql0", "ql1")
    order["T"] += [("c", 0), ("c", 1)]
    for s in range(NB):
        order["S"].append(("s", s))
        order["O"].append(("o", s))
        if s < NB - 2:
            order["T"].append(("c", s + 2))
        order["T"].append(("p", s))
    order["T"] += [("k", 0), ("q", 0)]
    for j in range(4):
        cyc(("v", j))
    order["S"].append("oa")
    for u in range(UNITS):
        h, i = divmod(u, 4)
        order["S"].append(("s", NB + u))
        if i == 0:
            order["O"].append(("oh", h))
        if i == 1 and h < HEADS - 1:
            order["T"].append(("k", h + 1))
        if i == 2 and h < HEADS - 1:
            order["T"].append(("q", h + 1))
        if 0 <= NB + u - CONV_OUT < TILES:
            order["T"].append(("cv", NB + u - CONV_OUT))
        order["T"].append(("p", NB + u))
    for g in range(2):
        for t in range(TILES):
            cyc(("y", t, g))
    for t in range(TILES):
        for g in range(2):
            cyc(("h", t, g))
    return {n: (b, i) for b, names in order.items() for i, n in enumerate(names)}


def build(nc, a):
    ctx = ExitStack()
    plan = shared_bank_plan()
    with ctx:
        def sb(name, shape, dt=F32):
            return ctx.enter_context(nc.sbuf_tensor(name, shape, dt))

        H = sb("H", [P, TILES, D])
        Y = H
        XHI = sb("XHI", [P, TILES, KT, P], F32R)
        XLO = sb("XLO", [P, TILES, KT, P], F32R)
        WR = sb("WR", [P, RAW, 2, 512])
        WHI = sb("WHI", [P, SPLIT, 2, 512], F32R)
        WLO = sb("WLO", [P, SPLIT, 2, 512], F32R)
        OTOK = sb("OTOK", [P, TILES, 512])
        PTR = sb("PTR", [P, 2, TOK])
        UT = sb("UT", [P, 4, STATE + SEQ])
        UTS = sb("UTS", [P, 4, NB, STATE + NS])
        VT = sb("VT", [P, 4 * TOK])
        VTv = VT[:, :].rearrange("p (t c e) -> p t c e", c=4, e=P)
        EMB = [[UT[:, t, STATE:] for t in range(TILES - 1)], []]
        WQ = sb("WQ", [P, 2, HEADS, 128])
        WKV = sb("WKV", [P, HEADS, 128])
        Z = sb("Z", [P, TILES, NZ + ROPE])
        CQT = sb("CQT", [P, 2, TOK])
        CKVT = sb("CKVT", [P, TOK])
        KRS = sb("KRS", [P, P])
        V = sb("V", [P, 4, 512])
        QL = V[:, 0:2, :].rearrange("p a (s h t) -> p (a s) h t", h=HEADS, t=NS)
        OL = sb("OL", [P, HEADS, P])
        UKT = OL
        EMB[0].append(UTS[:, :, :, :].rearrange("p c b j -> p (c b j)")[:, 0:512])
        EMB[1] += [OTOK[:, t, :] for t in range(TILES)]
        KH = sb("KH", [P, 2, 512])
        QH = sb("QH", [P, 2, 512])
        QS = QH[:, :, :].rearrange("p a (s h t) -> p (a s) h t", h=HEADS, t=NS)
        SB = sb("SB", [P, 2, 512])
        PT = sb("PT", [P, 2, 4, P])
        CKV = V[:, 2:4, :].rearrange("p a (b j r) -> p (a b) j r", b=2, r=LORA)
        CKR = sb("CKR", [P, CACHED, 2, 128])
        CTK = sb("CTK", [P, 512])
        TH = sb("TH", [P, 2, 512])
        ROWS = VT[0:30, 1536:1536 + P]
        GT = sb("GT", [P, 30])
        CWT = sb("CWT", [P, 4, TAPS])
        LNKV = sb("LNKV", [P, LORA])
        LCG = sb("LCG", [P, CH])[:, :]
        LCB = CTK[:, :]
        IDENT = sb("IDENT", [P, P])
        ROPET = sb("ROPET", [P, TOK])
        ROPEK = sb("ROPEK", [P, TILES, 4, 16])
        MASK = sb("MASK", [P, 512], BF16)
        MROW = sb("MROW", [1, 240])
        ONES = sb("ONES", [1, P])
        JUNK = sb("JUNK", [P, D], BF16)
        MS = sb("MS", [P, 32])
        RS = sb("RS", [P, 32])
        HR = sb("HR", [P, 8])
        NR = sb("NR", [P, 3, 16])
        RSV = sb("RSV", [P, TILES])
        KRA = SB[:, 0, 0:32 * TILES].rearrange("p (t a e) -> p t a e", t=TILES, a=2)
        KRB = SB[:, 1, 0:32 * TILES].rearrange("p (t a e) -> p t a e", t=TILES, a=2)
        NBIAS = sb("NBIAS", [P, NB + UNITS])
        SUMS = sb("SUMS", [P, NB + UNITS])
        RSUM = sb("RSUM", [P, NB + UNITS])
        BN6 = sb("BN6", [P, TILES, 6])
        MV = sb("MV", [P, TILES, 2])

        G_IN, G_PG, G_OUT, G_Q, G_CB = 0, 8, 16, 24, 26

        acc = [ctx.enter_context(nc.psum_tensor(f"acc{t}", [P, 512], F32)) for t in range(TILES)]
        shared = {b: ctx.enter_context(nc.psum_tensor(f"shared{b}", [P, 512], F32)) for b in "STO"}

        sems = []

        def sem(name):
            s = ctx.enter_context(nc.semaphore(name))
            sems.append(s)
            return s

        def kept(name):
            return ctx.enter_context(nc.semaphore(name))

        ident_in = kept("ident_in")
        tables_in = kept("tables_in")
        rows_in = kept("rows_in")
        taps_in = kept("taps_in")
        state_in = kept("state_in")
        wkv_in = kept("wkv_in")
        h_first = [kept(f"h_first{t}") for t in range(TILES)]
        w_first = [kept(f"w_first{i}") for i in range(RAW)]

        filled = {b: sem(f"filled_{b}") for b in "STO"}
        drained = {b: sem(f"drained_{b}") for b in "STO"}
        acc_filled = [sem(f"acc_filled{t}") for t in range(TILES)]
        acc_drained = [sem(f"acc_drained{t}") for t in range(TILES)]
        w_loaded = [sem(f"w_loaded{i}") for i in range(RAW)]
        hi_ready = sem("hi_ready")
        split_ready = sem("split_ready")
        piece_used = sem("piece_used")
        half_hi = sem("half_hi")
        spilled = sem("spilled")
        h_in = [sem(f"h_in{half}") for half in range(2)]
        p_in = sem("p_in")
        wq_rot = sem("wq_rot")
        lnconv_in = sem("lnconv_in")
        cache_in = [sem(f"cache_in{i}") for i in range(CACHED)]
        squares = sem("squares")
        rstd_ready = sem("rstd_ready")
        cq_scaled = sem("cq_scaled")
        latents_ready = sem("latents_ready")
        gated = sem("gated")
        exped = sem("exped")
        p_scaled = sem("p_scaled")
        conv_done = [sem(f"conv_done{half}") for half in range(2)]
        ln_scaled = sem("ln_scaled")
        ln_done = sem("ln_done")
        stats_ready = sem("stats_ready")
        v_tanh = sem("v_tanh")
        ya_ready = sem("ya_ready")
        yc_ready = sem("yc_ready")
        ya_scaled = sem("ya_scaled")
        yc_scaled = sem("yc_scaled")
        h_done = sem("h_done")
        latents_stored = sem("latents_stored")
        u_stored = sem("u_stored")
        states_stored = sem("states_stored")
        dve_chain = sem("dve_chain")
        act_chain = sem("act_chain")
        const_set = sem("const_set")
        next_in = sem("next_in")
        wq_in = sem("wq_in")
        lnkv_in = sem("lnkv_in")
        final_in = sem("final_in")
        y_stored = sem("y_stored")

        def bank(name):
            return shared[plan[name][0]]

        def fill_wait(eng, name):
            b, i = plan[name]
            if i:
                eng.wait_ge(drained[b], i)

        def fill_inc(ins, name):
            ins.then_inc(filled[plan[name][0]], 1)

        def filled_wait(eng, name):
            b, i = plan[name]
            eng.wait_ge(filled[b], i + 1)

        def drain_inc(ins, name):
            ins.then_inc(drained[plan[name][0]], 1)

        def copied_wait(eng, name):
            b, i = plan[name]
            eng.wait_ge(drained[b], i + 1)

        class Chain:

            def __init__(self, eng, s):
                self.eng, self.s, self.n = eng, s, 0

            def link(self, ins):
                self.n += 1
                ins.then_inc(self.s, 1)
                self.eng.wait_ge(self.s, self.n)

        def rsqrt(eng, chain, src, dst, n):
            half = NR[:, 0, 0:n]
            tmp = NR[:, 1, 0:n]
            x = NR[:, 2, 0:n]
            chain.link(eng.tensor_scalar(x, src, EPS, None, ALU.add))
            chain.link(eng.tensor_scalar(half, x, -0.5, None, ALU.mult))
            chain.link(eng.tensor_scalar(dst.bitcast(I32), x.bitcast(I32), -0.5, MAGIC, ALU.mult, ALU.add))
            for k in range(3):
                chain.link(eng.tensor_tensor(tmp, dst, dst, ALU.mult))
                chain.link(eng.tensor_tensor(tmp, tmp, half, ALU.mult))
                last = eng.scalar_tensor_tensor(out=dst, in0=tmp, scalar=1.5, in1=dst, op0=ALU.add, op1=ALU.mult)
                if k < 2:
                    chain.link(last)
            return last

        def part_used(eng, i):
            name, c = PARTS[i]
            if c == 3:
                eng.wait_ge(acc_filled[TILES - 1], BLK[name] + 1)
            else:
                eng.wait_ge(piece_used, sum(x != 3 for _, x in PARTS[:i + 1]))

        def gain_column(i, k):
            name, c = PARTS[i]
            col = G_IN if name in ZCOL else G_OUT if name[0] == "o" else G_PG
            return GT[:, col + 2 * c + k:col + 2 * c + k + 1]

        def width(name):
            return NZ if name == "zA" else 512

        def raw_slot(i):
            j = CHUNKS.index(PARTS[i])
            return j, WR[:, j % RAW, :, 0:width(PARTS[i][0])]

        spill = nc.dram_tensor("residual_spill", (P, TILES, D), F32, kind="Internal").ap()

        def transfers(j):
            return 2 if CHUNKS[j][0][0] == "u" else 1

        def raw_wait(eng, j):
            if j < RAW:
                eng.wait_ge(w_first[j], 16 * transfers(j))
            else:
                eng.wait_ge(w_loaded[j % RAW], 16 * sum(transfers(x) for x in range(j % RAW + RAW, j + 1, RAW)))

        def load_piece(sp, index, j, signal):
            name, c = CHUNKS[j]
            if name in ZCOL:
                w, (col, n) = "w_in", ZCOL[name]
            else:
                w, col, n = {"o": "w_out", "e": "w_pe", "g": "w_pg"}[name[-2]], 512 * int(name[-1]), 512
            if name[0] == "u":
                src = a[w][bass.ds(index, 1), 2 * P * c:2 * P * (c + 1), NZ + 512:NZ + 1536]
                src = src.rearrange("o (k p) (g n) -> p (o k) g n", p=P, g=2)[:, :, :, col - NZ - 512:col - NZ - 256]
                for k in range(2):
                    sp.dma_start(WR[:, j % RAW, k, :].rearrange("p (g n) -> p g n", g=2), src[:, k]).then_inc(signal, 16)
                return
            src = a[w][bass.ds(index, 1), 2 * P * c:2 * P * (c + 1), col:col + n]
            sp.dma_start(WR[:, j % RAW, :, 0:n], src.rearrange("o (k p) n -> p (o k) n", p=P)).then_inc(signal, 16)

        def load_rows(sp, index, signal):
            for name, g, n in (("ln_in", G_IN, 8), ("ln_pg", G_PG, 8), ("ln_out_a", G_OUT, 4),
                               ("ln_out_c", G_OUT + 4, 4), ("ln_q", G_Q, 2), ("conv_b", G_CB, 4)):
                sp.dma_start(ROWS[g:g + n, :], a[name][bass.ds(index, 1)].rearrange("o (k p) -> (o k) p", p=P)).then_inc(signal, 16)

        def load_taps(sp, index, signal):
            sp.dma_start(VT[0:TAPS, 1024:1536], a["conv_w"][bass.ds(index, 1)].rearrange("o k c -> (o k) c")).then_inc(signal, 16)

        def load_state(sp, index, signal):
            sp.dma_start(VT[0:120, 0:1024].rearrange("p (a c) -> p a c", a=2),
                         a["state_conv"][bass.ds(index, 1)].rearrange("o (a b) j c -> (b j) (o a) c", a=2)).then_inc(signal, 16)

        def load_wkv(sp, index, signal):
            sp.dma_start(WKV[:, :, :], a["w_kv_b"][bass.ds(index, 1)].rearrange("o r (h e) -> (o r) h e", e=128)).then_inc(signal, 16)

        def load_wq(sp, index, signal):
            for k in range(2):
                sp.dma_start(WQ[:, k, :, 0:NOPE + ROPE],
                             a["w_q_b"][bass.ds(index, 1), P * k:P * (k + 1), :].rearrange("o p (h e) -> (o p) h e", h=HEADS)).then_inc(signal, 16)

        def load_lnkv(sp, index, signal):
            sp.dma_start(LNKV[:, :], a["ln_kv"][bass.ds(index, 1)].to_broadcast([P, LORA])).then_inc(signal, 16)

        def load_cache(pool, index, s, signal):
            slot = s % CACHED
            src = a["cache_ckv"][bass.ds(index, 1), s]
            pool.dma_start(CKV[:, slot, :, :], src.rearrange("o (j p) r -> p (o j) r", p=P)).then_inc(signal, 16)
            src = a["cache_krope"][bass.ds(index, 1), s].rearrange("o (j p) r -> p (o j) r", p=P)
            for k in range(2):
                lo = NOPE + ROPE * k
                pool.dma_start(CKR[:, slot, :, lo:lo + ROPE], src).then_inc(signal, 16)

        with nc.Block() as block:
            @block.sync
            def _(sp):
                sp.dma_start(IDENT[:, :], a["c_ident"]).then_inc(ident_in, 16)
                sp.dma_start(MROW[:, :], a["c_mrow"]).then_inc(tables_in, 16)

                def residual(t):
                    src = a["x_prompt"][0, P * t:P * (t + 1), :] if t < 4 else a["x_sample"].rearrange("b s d -> (b s) d")
                    sp.dma_start(H[:, t, :], src).then_inc(h_first[t], 16)

                residual(0)
                load_piece(sp, 0, 0, w_first[0])
                residual(1)
                residual(2)
                load_piece(sp, 0, 1, w_first[1])
                residual(3)
                residual(4)
                sp.dma_start(ROPET[:, :], a["c_ropet"]).then_inc(tables_in, 16)
                sp.dma_start(ROPEK[:, :, :, :], a["c_ropek"]).then_inc(tables_in, 16)
                load_taps(sp, 0, taps_in)
                load_wkv(sp, 0, wkv_in)
                load_piece(sp, 0, 2, w_first[2])
                load_state(sp, 0, state_in)

            @block.scalar
            def _(act):
                load_rows(act, 0, rows_in)

            @block.gpsimd
            def _(pool):
                nc.gpsimd.memset(UT[:, :, 0:STATE], 0.0).then_inc(const_set, 1)
                nc.gpsimd.memset(CKR[:, :, :, 0:NOPE], 0.0).then_inc(const_set, 1)
                nc.gpsimd.memset(ONES[:, :], 1.0).then_inc(const_set, 1)
                nc.gpsimd.memset(MASK[:, :], 0.0).then_inc(const_set, 1)
                pool.wait_ge(const_set, 4)
                nc.gpsimd.memset(MASK[0:P // 2, 512 - P // 2:512], NEG).then_inc(const_set, 1)

        with nc.Fori(0, DEPTH) as layer:
            def at(name):
                return a[name][bass.ds(layer, 1)]

            with nc.Block() as block:
                @block.sync
                def _(sp):
                    def piece(j):
                        before = CHUNKS[j - RAW]
                        if before in PART:
                            sp.wait_ge(split_ready, PART[before] + 1)
                        else:
                            sp.wait_ge(acc_filled[TILES - 1], BLK[before[0]] + 1)
                        load_piece(sp, layer, j, w_loaded[j % RAW])

                    sp.dma_start(OTOK[:, 0:4, 0:PLE], at("p_prompt").rearrange("l o (t p) d -> p (l o t) d", p=P)).then_inc(p_in, 16)
                    sp.dma_start(OTOK[:, 4, 0:PLE], at("p_sample").rearrange("o b s d -> (o b s) d")).then_inc(p_in, 16)
                    back = CHUNKS.index(("o0", 3)) + 1
                    for j in range(RAW, RAW + 2):
                        piece(j)
                    load_wq(sp, layer, wq_in)
                    load_lnkv(sp, layer, lnkv_in)
                    for t in range(TILES):
                        sp.wait_ge(h_first[t], 16)
                    sp.dma_start(spill, H[:, :, :]).then_inc(spilled, 16)
                    for j in range(RAW + 2, back):
                        piece(j)
                    sp.wait_ge(spilled, 16)
                    for half in range(2):
                        cols = slice(512 * half, 512 * (half + 1))
                        for t in range(TILES):
                            filled_wait(sp, ("y", t, half))
                            sp.dma_start(H[:, t, cols], spill[:, t, cols]).then_inc(h_in[half], 16)
                        if half == 0:
                            piece(back)
                            back += 1
                    following = (layer + 1) % DEPTH
                    early = [load_rows, load_taps, load_state, load_wkv]
                    for j in range(back, len(CHUNKS)):
                        piece(j)
                        if early and j >= back + 3:
                            early.pop(0)(sp, following, next_in)
                    sp.wait_ge(split_ready, len(PARTS))
                    for j in range(RAW):
                        load_piece(sp, following, j, next_in)
                    sp.wait_ge(next_in, 16 * (6 + 1 + 1 + 1 + sum(transfers(j) for j in range(RAW))))

                @block.tensor
                def _(pe):
                    mm = nc.tensor.matmul

                    def flip(out, in_):
                        rows = in_.shape[0]
                        return nc.tensor.transpose(out, in_, IDENT[0:rows, 0:rows])

                    def quad(name):
                        return bank(name)[:, :].rearrange("p (j t) -> p j t", t=P)

                    pe.wait_ge(ident_in, 16)
                    fill_wait(pe, "gain")
                    pe.wait_ge(rows_in, 16 * 6)
                    fill_inc(flip(bank("gain")[:, 0:30], ROWS[:, :]), "gain")

                    def flip_half(name, src):
                        g = name[2]
                        fill_wait(pe, name)
                        for j in range(4):
                            last = flip(quad(name)[:, j, :], src[:, P * (4 * g + j):P * (4 * g + j + 1)])
                        fill_inc(last, name)

                    for t in range(TILES):
                        pe.wait_ge(h_first[t], 16)
                        for g in range(2):
                            flip_half(("x", t, g), H[:, t, :])
                    def turn_small():
                        fill_wait(pe, "taps")
                        pe.wait_ge(taps_in, 16)
                        for c in range(4):
                            last = flip(bank("taps")[:, TAPS * c:TAPS * (c + 1)], VT[0:TAPS, 1024 + P * c:1024 + P * (c + 1)])
                        fill_inc(last, "taps")
                        pe.wait_ge(wkv_in, 16)
                        for g in range(2):
                            name = f"uk{g}"
                            fill_wait(pe, name)
                            for j in range(4):
                                last = flip(quad(name)[0:NOPE, j, :], WKV[:, 4 * g + j, 0:NOPE])
                            fill_inc(last, name)
                        pe.wait_ge(state_in, 16)
                        for g in range(2):
                            name = f"st{g}"
                            fill_wait(pe, name)
                            for c in range(4):
                                last = flip(bank(name)[:, 120 * c:120 * (c + 1)], VT[0:120, 512 * g + P * c:512 * g + P * (c + 1)])
                            fill_inc(last, name)

                    def turn_embeddings():
                        pe.wait_ge(p_in, 32)
                        for g in range(3):
                            name = f"p{g}"
                            fill_wait(pe, name)
                            for j, t in enumerate(range(2 * g, min(2 * g + 2, TILES))):
                                for k in range(2):
                                    last = flip(quad(name)[:, 2 * j + k, :], OTOK[:, t, P * k:P * (k + 1)])
                            fill_inc(last, name)

                    def quantum(name, c, t):
                        i = PART[(name, c)]
                        n = width(name)
                        first, final = c == 0, c == 3
                        if t == 0:
                            pe.wait_ge(split_ready, i + 1)
                        if first and BLK[name]:
                            pe.wait_ge(acc_drained[t], BLK[name])
                        for k in range(2):
                            hi, lo = XHI[:, t, 2 * c + k, :], XLO[:, t, 2 * c + k, :]
                            w_hi, w_lo = WHI[:, i % SPLIT, k, 0:n], WLO[:, i % SPLIT, k, 0:n]
                            out = acc[t][:, 0:n]
                            mm(out, hi, w_hi, start=(first and k == 0), stop=False)
                            mm(out, hi, w_lo, start=False, stop=False)
                            last = mm(out, lo, w_hi, start=False, stop=(final and k == 1))
                        if final:
                            last.then_inc(acc_filled[t], 1)
                        elif t == TILES - 1:
                            last.then_inc(piece_used, 1)

                    def turn_u(half):
                        for t in range(TILES):
                            name = ("u", half, t)
                            fill_wait(pe, name)
                            pe.wait_ge(gated, TILES * half + t + 1)
                            for b in range(2):
                                col = 512 + 256 * half + P * b
                                last = flip(quad(name)[:, b, :], Y[:, t, col:col + P])
                            fill_inc(last, name)

                    for name in ("u0", "u1", "zA"):
                        for c in range(4):
                            for t in range(TILES):
                                if name == "u0":
                                    copied_wait(pe, ("x", t, c // 2))
                                quantum(name, c, t)
                            if c == 0 and name == "u0":
                                turn_small()
                            if c == 1 and name == "u0":
                                turn_embeddings()
                            if c == 1 and name != "u0":
                                turn_u(int(name == "zA"))
                    for q in range(EARLY):
                        quantum(*QUANTA[q])

                    pe.wait_ge(latents_ready, 1)
                    for t in range(TILES):
                        name = ("small", t)
                        fill_wait(pe, name)
                        pe.wait_ge(cq_scaled, t + 1)
                        for k in range(2):
                            flip(quad(name)[:, k, :], Z[:, t, P * k:P * (k + 1)])
                        flip(quad(name)[:, 2, :], Z[:, t, QLORA:QLORA + LORA])
                        fill_inc(flip(quad(name)[:, 3, :], Z[:, t, NZ + ROPE - P:NZ + ROPE]), name)

                    pe.wait_ge(wq_rot, 2)
                    pe.wait_ge(wq_in, 32)
                    for t in range(TILES):
                        copied_wait(pe, ("small", t))
                    for g in range(2):
                        name = f"qs{g}"
                        fill_wait(pe, name)
                        for j in range(4):
                            for k in range(2):
                                last = mm(quad(name)[:, j, :], WQ[:, k, 4 * g + j, :], CQT[:, k, SEQ:TOK],
                                          start=(k == 0), stop=(k == 1))
                        fill_inc(last, name)
                    copied_wait(pe, "uk0")
                    copied_wait(pe, "uk1")
                    for g in range(2):
                        name = f"ql{g}"
                        fill_wait(pe, name)
                        copied_wait(pe, f"qs{g}")
                        for j in range(4):
                            last = mm(quad(name)[:, j, :], UKT[0:NOPE, 4 * g + j, :], QS[0:NOPE, :, 4 * g + j, :],
                                      start=True, stop=True)
                        fill_inc(last, name)
                    def filler(n):
                        if n in FILL:
                            quantum(*QUANTA[FILL[n]])

                    def embed(half, t):
                        if t == 0:
                            raw_wait(pe, CHUNKS.index((f"pe{half}", 0)))
                        pe.wait_ge(acc_drained[t], BLK["pe0"] + half)
                        slot = CHUNKS.index((f"pe{half}", 0)) % RAW
                        for k in range(2):
                            last = mm(acc[t][:, :], PTR[:, k, P * t:P * (t + 1)], WR[:, slot, k, :],
                                      start=(k == 0), stop=(k == 1))
                        last.then_inc(acc_filled[t], 1)

                    def flip_cache(s):
                        name = ("c", s)
                        fill_wait(pe, name)
                        slot = s % CACHED
                        pe.wait_ge(cache_in[slot], 48 * (s // CACHED + 1))
                        for j in range(2):
                            flip(quad(name)[:, j, :], CKV[:, slot, j, :])
                            last = flip(quad(name)[:, 2 + j, :], CKR[:, slot, j, :])
                        fill_inc(last, name)

                    def flip_probs(n, w):
                        name = ("p", n)
                        fill_wait(pe, name)
                        for j in range(w // P):
                            last = flip(quad(name)[:, j, :], SB[:, n % 2, P * j:P * (j + 1)])
                        fill_inc(last, name)

                    def sample_values(s):
                        name = ("o", s)
                        fill_wait(pe, name)
                        copied_wait(pe, ("p", s))
                        out = bank(name)[:, 0:P]
                        for j in range(2):
                            mm(out, CKV[:, s % CACHED, j, :], PT[:, s % 2, j, :], start=(j == 0), stop=False)
                        fill_inc(mm(out, Z[:, TILES - 1, QLORA:QLORA + LORA], PT[:, s % 2, 2, :],
                                    start=False, stop=True), name)

                    def sample_scores(s):
                        name = ("s", s)
                        fill_wait(pe, name)
                        copied_wait(pe, ("c", s))
                        q_lat = QL[:, s, :, :].rearrange("p h t -> p (h t)")
                        q_rot = QS[NOPE:P, s, :, :].rearrange("p h t -> p (h t)")
                        mm(bank(name)[:, 0:PAST], q_lat, CTK[:, 0:PAST], start=True, stop=False)
                        mm(bank(name)[:, 0:PAST], q_rot, CTK[NOPE:P, PAST:2 * PAST], start=False, stop=True)
                        new = bank(name)[:, PAST:PAST + P]
                        mm(new, q_lat, CKVT[:, SEQ:TOK], start=True, stop=False)
                        mm(new, q_rot, KRS[NOPE:P, :], start=False, stop=False)
                        fill_inc(mm(new, ONES[:, :], MROW[:, 112 - NS * s:240 - NS * s], start=False, stop=True), name)

                    copied_wait(pe, "ql1")
                    pe.wait_ge(tables_in, 16 * 3)
                    flip_cache(0)
                    sample_scores(0)
                    flip_cache(1)
                    for s in range(NB):
                        if s < NB - 1:
                            sample_scores(s + 1)
                        if s:
                            sample_values(s - 1)
                        if s < NB - 2:
                            flip_cache(s + 2)
                        filler(s)
                        pe.wait_ge(p_scaled, s + 1)
                        flip_probs(s, PAST + P)

                    def keys(h):
                        name = ("k", h)
                        fill_wait(pe, name)
                        fill_inc(mm(bank(name)[0:NOPE, :], WKV[:, h, 0:NOPE], CKVT[:, 0:SEQ], start=True, stop=True), name)

                    def queries(h):
                        name = ("q", h)
                        fill_wait(pe, name)
                        for k in range(2):
                            last = mm(bank(name)[:, :], WQ[:, k, h, :], CQT[:, k, 0:SEQ], start=(k == 0), stop=(k == 1))
                        fill_inc(last, name)

                    def scores(u):
                        h, i = divmod(u, 4)
                        name = ("s", NB + u)
                        fill_wait(pe, name)
                        if i == 0:
                            copied_wait(pe, ("k", h))
                            copied_wait(pe, ("q", h))
                        w = P * (i + 1)
                        fill_inc(mm(bank(name)[:, 0:w], QH[:, h % 2, P * i:P * (i + 1)], KH[:, h % 2, 0:w],
                                    start=True, stop=True), name)

                    def values(u):
                        h, i = divmod(u, 4)
                        n = NB + u
                        name = ("oh", h)
                        if i == 0:
                            fill_wait(pe, name)
                        copied_wait(pe, ("p", n))
                        for j in range(i + 1):
                            last = mm(quad(name)[:, i, :], PT[:, n % 2, j, :], V[:, j, P * (h // 2):P * (h // 2 + 1)],
                                      start=(j == 0), stop=(j == i))
                        if i == 3:
                            fill_inc(last, name)

                    keys(0)
                    queries(0)
                    sample_values(NB - 1)
                    for j in range(4):
                        name = ("v", j)
                        fill_wait(pe, name)
                        fill_inc(mm(bank(name)[:, :], CKVT[:, P * j:P * (j + 1)], WKV[:, :, NOPE:P], start=True, stop=True), name)
                    fill_wait(pe, "oa")
                    copied_wait(pe, ("o", NB - 1))
                    for h in range(HEADS):
                        last = mm(bank("oa")[:, VH * h:VH * (h + 1)], OL[:, h, :], WKV[:, h, NOPE:P], start=True, stop=True)
                    fill_inc(last, "oa")
                    for j in range(4):
                        copied_wait(pe, ("v", j))
                    scores(0)
                    for u in range(UNITS):
                        h, i = divmod(u, 4)
                        if u < UNITS - 1:
                            scores(u + 1)
                        if u:
                            values(u - 1)
                        if i == 1 and h < HEADS - 1:
                            keys(h + 1)
                        if i == 2 and h < HEADS - 1:
                            queries(h + 1)
                        filler(NB + u)
                        if 0 <= u - EMBED < TILES:
                            if u == EMBED:
                                copied_wait(pe, "p2")
                            embed(0, u - EMBED)
                        t = NB + u - CONV_OUT
                        if 0 <= t < TILES:
                            name = ("cv", t)
                            fill_wait(pe, name)
                            for half in range(2):
                                pe.wait_ge(conv_done[half], 4 * TAPS)
                            for c in range(4):
                                last = flip(quad(name)[:, c, :], VTv[:, t, c, :])
                            fill_inc(last, name)
                        pe.wait_ge(exped, NB + u + 1)
                        flip_probs(NB + u, P * (i + 1))
                    values(UNITS - 1)

                    for t in range(TILES):
                        embed(1, t)
                    for g in range(2):
                        for t in range(TILES):
                            pe.wait_ge((ya_scaled, yc_scaled)[g], t + 1)
                            flip_half(("y", t, g), Y[:, t, :])
                        for c in (2 * g, 2 * g + 1):
                            for t in range(TILES):
                                copied_wait(pe, ("y", t, g))
                                quantum("o0", c, t)

                    def flip_h(t):
                        pe.wait_ge(acc_drained[t], BLK["o1"] + 1)
                        for g in range(2):
                            flip_half(("h", t, g), H[:, t, :])

                    for c in range(4):
                        for t in range(TILES):
                            quantum("o1", c, t)
                            if c == 3 and t >= 3:
                                flip_h(t - 3)
                    for t in range(TILES - 3, TILES):
                        flip_h(t)
                    for name in ("pg0", "pg1"):
                        for c in range(4):
                            for t in range(TILES):
                                if name == "pg0":
                                    copied_wait(pe, ("h", t, c // 2))
                                quantum(name, c, t)

                @block.scalar
                def _(act):
                    av = nc.scalar.activation
                    th = [0]
                    n_sq = [0]

                    def mean_square(src, col, n, scale=1.0):
                        if n_sq[0]:
                            act.wait_ge(squares, n_sq[0])
                        n_sq[0] += 1
                        av(JUNK[:, 0:n], src, ACT.Square, scale=scale * n ** -0.5,
                           accum_out=MS[:, col:col + 1]).then_inc(squares, 1)

                    def copy(out, in_, scale=None):
                        return av(out, in_, ACT.Copy) if scale is None else av(out, in_, ACT.Copy, scale=scale)

                    def quad(name):
                        return bank(name)[:, :].rearrange("p (j t) -> p j t", t=P)

                    def high(i):
                        j, raw = raw_slot(i)
                        raw_wait(act, j)
                        if i >= SPLIT:
                            part_used(act, i - SPLIT)
                        for k in range(2):
                            last = copy(WHI[:, i % SPLIT, k, 0:width(PARTS[i][0])], raw[:, k, :], gain_column(i, k))
                        last.then_inc(hi_ready, 1)

                    def high_half(name):
                        _, t, g = name
                        filled_wait(act, name)
                        copy(XHI[:, t, 4 * g:4 * g + 4, :], quad(name)).then_inc(half_hi, 1)

                    copied_wait(act, "gain")
                    for t in range(TILES):
                        for g in range(2):
                            high_half(("x", t, g))
                        if t < 2:
                            high(t)
                    for t in range(TILES):
                        act.wait_ge(h_first[t], 16)
                        mean_square(H[:, t, :], t, D)
                    high(2)
                    for g in range(2):
                        name = f"uk{g}"
                        filled_wait(act, name)
                        drain_inc(copy(UKT[0:NOPE, 4 * g:4 * g + 4, :], quad(name)[0:NOPE, :, :]), name)
                    for g in range(2):
                        name = f"st{g}"
                        filled_wait(act, name)
                        for c in range(4):
                            last = copy(UTS[:, c, 4 * g:4 * g + 4, 0:STATE],
                                        bank(name)[:, 120 * c:120 * (c + 1)].rearrange("p (b j) -> p b j", b=4))
                        drain_inc(last, name)
                    high(3)
                    for g in range(3):
                        name = f"p{g}"
                        filled_wait(act, name)
                        m = min(2, TILES - 2 * g)
                        for k in range(2):
                            src = bank(name)[:, 0:2 * P * m].rearrange("p (t k e) -> p k t e", k=2, e=P)[:, k]
                            last = copy(PTR[:, k, 2 * P * g:2 * P * g + P * m].rearrange("p (t e) -> p t e", e=P), src)
                        drain_inc(last, name)

                    act.wait_ge(wq_in, 32)
                    copy(WQ[:, :, :, 96:112], WQ[:, :, :, 80:96]).then_inc(wq_rot, 1)
                    copy(WQ[:, :, :, 112:128], WQ[:, :, :, 64:80]).then_inc(wq_rot, 1)

                    def tanh_acc(t, block_no, hr):
                        k = th[0]
                        th[0] += 1
                        if k >= 2:
                            act.wait_ge(gated, k - 1)
                        av(TH[:, k % 2, :], acc[t][:, :], ACT.Tanh, scale=hr).then_inc(acc_drained[t], 1)

                    def leave(part, copy_out):
                        high(part)
                        for t in range(TILES):
                            copy_out(t)
                            if t == 1:
                                high(part + 1)

                    def u_out(half, t):
                        name = f"u{half}"
                        act.wait_ge(acc_filled[t], BLK[name] + 1)
                        col = 512 + 256 * half
                        copy(Y[:, t, col:col + 256], acc[t][:, 0:256], HR[:, t:t + 1])
                        k = th[0]
                        th[0] += 1
                        if k >= 2:
                            act.wait_ge(gated, k - 1)
                        av(TH[:, k % 2, 0:256], acc[t][:, 256:512], ACT.Tanh, scale=HR[:, t:t + 1]).then_inc(acc_drained[t], 1)

                    def turned_u_out(half):
                        for t in range(TILES):
                            name = ("u", half, t)
                            filled_wait(act, name)
                            if t < TILES - 1:
                                last = copy(UT[:, 2 * half:2 * half + 2, STATE + P * t:STATE + P * (t + 1)], quad(name)[:, 0:2, :])
                            else:
                                for c in range(2):
                                    last = copy(UTS[:, 2 * half + c, :, STATE:STATE + NS],
                                                quad(name)[:, c, :].rearrange("p (b j) -> p b j", b=NB))
                            drain_inc(last, name)

                    def latent_out(t):
                        act.wait_ge(acc_filled[t], BLK["zA"] + 1)
                        copy(Z[:, t, 0:NZ], acc[t][:, 0:NZ], RS[:, t:t + 1]).then_inc(acc_drained[t], 1)

                    act.wait_ge(rstd_ready, 1)
                    act.wait_ge(spilled, 16)
                    leave(4, lambda t: u_out(0, t))
                    high(6)
                    high(7)
                    turned_u_out(0)
                    leave(8, lambda t: u_out(1, t))
                    high(10)
                    high(11)
                    turned_u_out(1)
                    leave(12, latent_out)
                    for t in range(TILES):
                        act.wait_ge(acc_drained[t], BLK["zA"] + 1)
                        mean_square(Z[:, t, 0:QLORA], 5 + t, QLORA)
                        mean_square(Z[:, t, QLORA:QLORA + LORA], 10 + t, LORA)
                    high(14)
                    act.wait_ge(rstd_ready, 2)
                    for t in range(TILES):
                        copy(Z[:, t, 0:QLORA], Z[:, t, 0:QLORA], RS[:, 5 + t:6 + t]).then_inc(cq_scaled, 1)
                    for t in range(TILES):
                        name = ("small", t)
                        filled_wait(act, name)
                        cols = slice(P * t, P * (t + 1))
                        for k in range(2):
                            copy(CQT[:, k, cols], quad(name)[:, k, :], GT[:, G_Q + k:G_Q + k + 1])
                        copy(CKVT[:, cols], quad(name)[:, 2, :])
                        if t < TILES - 1:
                            copy(KH[NOPE:P, 0, cols], quad(name)[NOPE:P, 3, :])
                            drain_inc(copy(KH[NOPE:P, 1, cols], quad(name)[NOPE:P, 3, :]), name)
                        else:
                            drain_inc(copy(KRS[NOPE:P, :], quad(name)[NOPE:P, 3, :]), name)

                    for g in range(2):
                        name = f"ql{g}"
                        filled_wait(act, name)
                        for j in range(4):
                            last = copy(QL[:, :, 4 * g + j, :], quad(name)[:, j, :].rearrange("p (s t) -> p s t", t=NS))
                        drain_inc(last, name)
                    high(15)

                    def filler_out(n):
                        if n in NEXT_PART:
                            high(NEXT_PART[n])
                        if n not in FILL:
                            return
                        name, c, t = QUANTA[FILL[n]]
                        if c < 3:
                            return
                        act.wait_ge(acc_filled[t], BLK[name] + 1)
                        if name == "gc" and t == 0:
                            act.wait_ge(u_stored, 16 * (1 + NB))
                        col = 0 if name == "ga" else 512
                        copy(Y[:, t, col:col + 512], acc[t][:, :], HR[:, t:t + 1])
                        tanh_acc(t, BLK[name], HR[:, t:t + 1])

                    def probs(n, w):
                        copied_wait(act, ("s", n))
                        av(SB[:, n % 2, 0:w], SB[:, n % 2, 0:w], ACT.Exp, scale=-1.0, bias=NBIAS[:, n:n + 1],
                           accum_out=SUMS[:, n:n + 1]).then_inc(exped, 1)

                    def probs_out(n, k):
                        name = ("p", n)
                        filled_wait(act, name)
                        drain_inc(copy(PT[:, n % 2, 0:k, :], quad(name)[:, 0:k, :]), name)

                    def cache_out(s):
                        name = ("c", s)
                        filled_wait(act, name)
                        drain_inc(copy(CTK[:, :], bank(name)[:, :]), name)

                    def sample_out(s):
                        name = ("o", s)
                        filled_wait(act, name)
                        drain_inc(copy(OL[:, :, NS * s:NS * (s + 1)],
                                       bank(name)[:, 0:P].rearrange("p (h t) -> p h t", h=HEADS)), name)

                    def keys_out(h):
                        name = ("k", h)
                        filled_wait(act, name)
                        drain_inc(copy(KH[0:NOPE, h % 2, :], bank(name)[0:NOPE, :]), name)

                    cache_out(0)
                    cache_out(1)
                    for s in range(NB):
                        probs(s, PAST + P)
                        if s:
                            sample_out(s - 1)
                        if s < NB - 2:
                            cache_out(s + 2)
                        filler_out(s)
                        probs_out(s, 3)

                    def embedding_out(half, t):
                        act.wait_ge(acc_filled[t], BLK["pe0"] + half + 1)
                        copy(EMB[half][t], acc[t][:, :]).then_inc(acc_drained[t], 1)

                    def v_tanh_out(t):
                        k = th[0]
                        th[0] += 1
                        act.wait_ge(gated, k - 1)
                        act.wait_ge(ln_done, t + 1)
                        av(TH[:, k % 2, :], VT[:, 512 * t:512 * (t + 1)], ACT.Tanh, scale=0.5).then_inc(v_tanh, 1)

                    keys_out(0)
                    sample_out(NB - 1)
                    for j in range(4):
                        name = ("v", j)
                        filled_wait(act, name)
                        drain_inc(copy(V[:, j, :], bank(name)[:, :]), name)
                    filled_wait(act, "oa")
                    drain_inc(copy(OTOK[:, TILES - 1, :], bank("oa")[:, :]), "oa")
                    for u in range(UNITS):
                        h, i = divmod(u, 4)
                        if i == 1 and h < HEADS - 1:
                            keys_out(h + 1)
                        probs(NB + u, P * (i + 1))
                        filler_out(NB + u)
                        t = NB + u - CONV_OUT
                        if 0 <= t < TILES:
                            name = ("cv", t)
                            filled_wait(act, name)
                            drain_inc(copy(VTv[:, t, :, :], quad(name)), name)
                        if 0 <= u - EMBED < TILES:
                            if u == EMBED:
                                for half in range(2):
                                    act.wait_ge(conv_done[half], 4 * TAPS)
                            embedding_out(0, u - EMBED)
                        probs_out(NB + u, i + 1)
                        if u >= UNITS - V_EARLY:
                            v_tanh_out(u - (UNITS - V_EARLY))

                    for t in range(TILES):
                        act.wait_ge(ya_ready, t + 1)
                        mean_square(Y[:, t, 0:512], 15 + t, 512)
                    v_tanh_out(2)
                    for t in range(TILES):
                        embedding_out(1, t)
                        if t == 1:
                            v_tanh_out(3)
                    high(21)
                    for t in range(TILES):
                        high_half(("y", t, 0))
                    v_tanh_out(4)
                    for t in range(TILES - 1):
                        act.wait_ge(yc_ready, t + 1)
                        mean_square(Y[:, t, 512:1024], 20 + t, 512)
                    act.wait_ge(yc_ready, TILES)
                    mean_square(Y[:, TILES - 1, 512:1024], 20 + TILES - 1, 512)
                    act.wait_ge(rstd_ready, 5)
                    for t in range(TILES):
                        copy(Y[:, t, 512:1024], Y[:, t, 512:1024], RS[:, 20 + t:21 + t]).then_inc(yc_scaled, 1)
                    high(22)
                    for t in range(TILES):
                        high_half(("y", t, 1))
                    high(23)
                    high(24)
                    high(25)
                    for i in range(26, 29):
                        high(i)
                    for t in range(TILES):
                        for g in range(2):
                            high_half(("h", t, g))
                        if t == 2:
                            high(29)
                    for t in range(TILES):
                        act.wait_ge(acc_drained[t], BLK["o1"] + 1)
                        mean_square(H[:, t, :], 25 + t, D)
                    high(30)
                    high(31)
                    act.wait_ge(rstd_ready, 6)

                    def pg_out(half, t):
                        act.wait_ge(acc_filled[t], BLK["pg0"] + half + 1)
                        tanh_acc(t, BLK["pg0"] + half, HR[:, t:t + 1])

                    leave(32, lambda t: pg_out(0, t))
                    high(34)
                    high(35)
                    for t in range(TILES):
                        pg_out(1, t)

                @block.vector
                def _(dve):
                    chain = Chain(dve, dve_chain)
                    tt, stt = nc.vector.tensor_tensor, nc.vector.scalar_tensor_tensor

                    def quad(name):
                        return bank(name)[:, :].rearrange("p (j t) -> p j t", t=P)

                    filled_wait(dve, "gain")
                    drain_inc(nc.vector.tensor_copy(GT[:, :], bank("gain")[:, 0:30]), "gain")
                    copied_wait(dve, "gain")

                    def low(i):
                        _, raw = raw_slot(i)
                        dve.wait_ge(hi_ready, i + 1)
                        for k in range(2):
                            at_k = (slice(None), i % SPLIT, k, slice(0, width(PARTS[i][0])))
                            last = stt(out=WLO[at_k], in0=raw[:, k, :], scalar=gain_column(i, k),
                                       in1=WHI[at_k].bitcast(F32), op0=ALU.mult, op1=ALU.subtract)
                        last.then_inc(split_ready, 1)

                    halves = [0]

                    def low_half(name):
                        _, t, g = name
                        halves[0] += 1
                        dve.wait_ge(half_hi, halves[0])
                        drain_inc(tt(XLO[:, t, 4 * g:4 * g + 4, :], quad(name), XHI[:, t, 4 * g:4 * g + 4, :].bitcast(F32),
                                     ALU.subtract), name)

                    for t in range(TILES):
                        for g in range(2):
                            low_half(("x", t, g))
                        if t < 2:
                            low(t)
                    filled_wait(dve, "taps")
                    drain_inc(nc.vector.tensor_copy(CWT[:, :, :], bank("taps")[:, 0:4 * TAPS].rearrange("p (c k) -> p c k", c=4)), "taps")
                    dve.wait_ge(squares, 5)
                    chain.link(rsqrt(dve, chain, MS[:, 0:5], RS[:, 0:5], 5))
                    nc.vector.tensor_scalar(HR[:, 0:5], RS[:, 0:5], 0.5, None, ALU.mult).then_inc(rstd_ready, 1)
                    for i in range(2, 5):
                        low(i)

                    k_th = [0]

                    def gate(out, other, ready, value):
                        k = k_th[0]
                        k_th[0] += 1
                        dve.wait_ge(ready, value)
                        return stt(out=out, in0=TH[:, k % 2, :], scalar=1.0, in1=other, op0=ALU.add, op1=ALU.mult)

                    def gated_u(half):
                        for t in range(TILES):
                            col = 512 + 256 * half
                            u = Y[:, t, col:col + 256]
                            dve.wait_ge(acc_drained[t], BLK[f"u{half}"] + 1)
                            stt(out=u, in0=TH[:, k_th[0] % 2, 0:256], scalar=1.0, in1=u, op0=ALU.add,
                                op1=ALU.mult).then_inc(gated, 1)
                            k_th[0] += 1
                            if t == 1:
                                low(5 + 4 * half)

                    def taps(place):
                        for k, half in place if isinstance(place, list) else TAP[place]:
                            n = 4 * k
                            for c in (2 * half, 2 * half + 1):
                                w = CWT[:, c, k:k + 1]
                                bias = GT[:, G_CB + c:G_CB + c + 1]
                                for part in range(2):
                                    if part == 0:
                                        out = VTv[:, 0:4, c, :]
                                        src = UT[:, c, k:k + SEQ].rearrange("p (t e) -> p t e", e=P)
                                    else:
                                        out = VTv[:, 4, c, :].rearrange("p (b j) -> p b j", b=NB)
                                        src = UTS[:, c, :, k:k + NS]
                                    if k == 0:
                                        ins = nc.vector.tensor_scalar(out, src, w, bias, ALU.mult, ALU.add)
                                    else:
                                        dve.wait_ge(conv_done[half], n - 3)
                                        ins = stt(out=out, in0=src, scalar=w, in1=out, op0=ALU.mult, op1=ALU.add)
                                    ins.then_inc(conv_done[half], 1)
                                    n += 1

                    gated_u(0)
                    low(6)
                    low(7)
                    for t in range(TILES):
                        copied_wait(dve, ("u", 0, t))
                    taps("u1a")
                    low(8)
                    taps("u1b")
                    gated_u(1)
                    taps("z0")
                    low(10)
                    taps("z1")
                    low(11)
                    taps("z2")
                    for t in range(TILES):
                        copied_wait(dve, ("u", 1, t))
                    taps("z3")
                    low(12)
                    taps("z4")
                    low(13)
                    taps("z5")

                    dve.wait_ge(squares, 15)
                    rsqrt(dve, chain, MS[:, 5:15], RS[:, 5:15], 10).then_inc(rstd_ready, 1)
                    dve.wait_ge(rstd_ready, 2)
                    dve.wait_ge(lnkv_in, 16)
                    dve.wait_ge(tables_in, 16 * 3)
                    for t in range(TILES):
                        lat = Z[:, t, QLORA:QLORA + LORA]
                        stt(out=lat, in0=lat, scalar=RS[:, 10 + t:11 + t], in1=LNKV[:, :], op0=ALU.mult, op1=ALU.mult)
                    kr = Z[:, :, NZ - ROPE:NZ].rearrange("p t (a e) -> p t a e", a=2)
                    tt(KRA[:, :, :, :], kr, ROPEK[:, :, 0:2, :], ALU.mult)
                    tt(KRB[:, :, 0, :], kr[:, :, 1, :], ROPEK[:, :, 2, :], ALU.mult)
                    chain.link(tt(KRB[:, :, 1, :], kr[:, :, 0, :], ROPEK[:, :, 3, :], ALU.mult))
                    kr2 = Z[:, :, NZ:NZ + ROPE].rearrange("p t (a e) -> p t a e", a=2)
                    tt(kr2, KRA[:, :, :, :], KRB[:, :, :, :], ALU.add)
                    tt(kr, KRA[:, :, :, :], KRB[:, :, :, :], ALU.add).then_inc(latents_ready, 1)

                    low(14)
                    taps("latents")
                    for g in range(2):
                        name = f"qs{g}"
                        filled_wait(dve, name)
                        rope = ROPET[:, SEQ:TOK].rearrange("p (s t) -> p s t", t=NS)
                        for j in range(4):
                            last = tt(QS[:, :, 4 * g + j, :], quad(name)[:, j, :].rearrange("p (s t) -> p s t", t=NS),
                                      rope, ALU.mult)
                        drain_inc(last, name)

                    low(15)
                    taps("queries")

                    def mask(n, w, add):
                        name = ("s", n)
                        filled_wait(dve, name)
                        drain_inc(nc.vector.tensor_tensor_reduce(SB[:, n % 2, 0:w], bank(name)[:, 0:w], add, -SCALE, 3e38,
                                                                 ALU.add, ALU.min, NBIAS[:, n:n + 1]), name)

                    def filler_gate(n):
                        if n in NEXT_PART:
                            low(NEXT_PART[n])
                        if n not in FILL:
                            return
                        name, c, t = QUANTA[FILL[n]]
                        if c == 3:
                            col = 0 if name == "ga" else 512
                            y = Y[:, t, col:col + 512]
                            gate(y, y, acc_drained[t], BLK[name] + 1).then_inc(gated, 1)

                    mask(0, PAST + P, MASK[:, 0:PAST + P])
                    for s in range(NB):
                        dve.wait_ge(exped, s + 1)
                        chain.link(nc.vector.reciprocal(RSUM[:, s:s + 1], SUMS[:, s:s + 1]))
                        nc.vector.tensor_scalar(SB[:, s % 2, 0:PAST + P], SB[:, s % 2, 0:PAST + P],
                                                RSUM[:, s:s + 1], None, ALU.mult).then_inc(p_scaled, 1)
                        if s < NB - 1:
                            mask(s + 1, PAST + P, MASK[:, 0:PAST + P])
                        taps(s)
                        filler_gate(s)

                    def queries_out(h):
                        name = ("q", h)
                        filled_wait(dve, name)
                        drain_inc(tt(QH[:, h % 2, :], bank(name)[:, :], ROPET[:, 0:SEQ], ALU.mult), name)

                    def head_out(h):
                        name = ("oh", h)
                        n = NB + 4 * h
                        dve.wait_ge(exped, n + 4)
                        chain.link(nc.vector.reciprocal(RSUM[:, n:n + 4], SUMS[:, n:n + 4]))
                        filled_wait(dve, name)
                        own = quad(name)[:, :, VH * (h % 2):VH * (h % 2 + 1)]
                        drain_inc(tt(OTOK[:, 0:4, VH * h:VH * (h + 1)], own,
                                     RSUM[:, n:n + 4].unsqueeze(2).to_broadcast([P, 4, VH]), ALU.mult), name)

                    def normed(t):
                        v = VT[:, 512 * t:512 * (t + 1)]
                        chain.link(nc.vector.tensor_scalar(v, v, MV[:, t, 0:1], RSV[:, t:t + 1], ALU.subtract, ALU.mult))
                        tt(v, v, LCG, ALU.mult).then_inc(ln_scaled, 1)

                    def layer_norm(n):
                        n -= CONV_OUT
                        if 0 <= n < TILES:
                            copied_wait(dve, ("cv", n))
                            nc.vector.bn_stats(BN6[:, n, :], VT[:, 512 * n:512 * (n + 1)]).then_inc(stats_ready, 1)
                        elif n == TILES:
                            dve.wait_ge(stats_ready, TILES)
                            for t in range(TILES):
                                last = nc.vector.bn_aggr(MV[:, t, :], BN6[:, t, :])
                            chain.link(last)
                            rsqrt(dve, chain, MV[:, :, 1], RSV[:, :], TILES).then_inc(rstd_ready, 1)
                        elif n == TILES + 1:
                            dve.wait_ge(rstd_ready, 3)
                            dve.wait_ge(lnconv_in, 32)
                            for t in range(2):
                                normed(t)
                        elif n > TILES + 1:
                            normed(n - TILES)

                    queries_out(0)
                    taps("turn")
                    mask(NB, P, MASK[:, 512 - P:512])
                    for u in range(UNITS):
                        h, i = divmod(u, 4)
                        if u < UNITS - 1:
                            w = P * ((i + 1) % 4 + 1)
                            mask(NB + u + 1, w, MASK[:, 512 - w:512])
                        taps(TAP[NB + u][:1])
                        if i == 0 and h:
                            head_out(h - 1)
                        if i == 2 and h < HEADS - 1:
                            queries_out(h + 1)
                        taps(TAP[NB + u][1:])
                        filler_gate(NB + u)
                        layer_norm(NB + u)
                    head_out(HEADS - 1)
                    copied_wait(dve, ("oh", HEADS - 1))
                    copied_wait(dve, "oa")
                    dve.wait_ge(gated, 4 * TILES)
                    for t in range(TILES):
                        y = Y[:, t, 0:512]
                        tt(y, y, OTOK[:, t, :], ALU.mult).then_inc(ya_ready, 1)

                    def conv_gate(t):
                        v = VT[:, 512 * t:512 * (t + 1)]
                        gate(v, v, v_tanh, t + 1).then_inc(gated, 1)
                        dve.wait_ge(gated, 4 * TILES + t + 1)
                        y = Y[:, t, 512:1024]
                        stt(out=y, in0=v, scalar=0.5, in1=y, op0=ALU.mult, op1=ALU.mult).then_inc(yc_ready, 1)

                    conv_gate(0)
                    conv_gate(1)
                    dve.wait_ge(squares, 20)
                    rsqrt(dve, chain, MS[:, 15:20], RS[:, 15:20], TILES).then_inc(rstd_ready, 1)
                    dve.wait_ge(rstd_ready, 4)
                    for t in range(TILES):
                        y = Y[:, t, 0:512]
                        nc.vector.tensor_scalar(y, y, RS[:, 15 + t:16 + t], None, ALU.mult).then_inc(ya_scaled, 1)
                    low(21)
                    for t in range(TILES):
                        low_half(("y", t, 0))
                    conv_gate(2)
                    conv_gate(3)
                    conv_gate(4)
                    dve.wait_ge(squares, 25)
                    rsqrt(dve, chain, MS[:, 20:25], RS[:, 20:25], TILES).then_inc(rstd_ready, 1)
                    low(22)
                    for t in range(TILES):
                        low_half(("y", t, 1))
                    low(23)
                    low(24)

                    def onto_residual(half, t):
                        dve.wait_ge(acc_filled[t], BLK["o0"] + half + 1)
                        hh = H[:, t, 512 * half:512 * (half + 1)]
                        tt(hh, hh, acc[t][:, :], ALU.add).then_inc(acc_drained[t], 1)

                    dve.wait_ge(h_in[0], 16 * TILES)
                    for t in range(TILES):
                        onto_residual(0, t)
                        if t == 1:
                            low(25)
                    for i in range(26, 29):
                        low(i)
                    dve.wait_ge(h_in[1], 16 * TILES)
                    for t in range(TILES):
                        onto_residual(1, t)
                        if t > 2:
                            for g in range(2):
                                low_half(("h", t - 3, g))
                    for t in range(TILES - 3, TILES):
                        for g in range(2):
                            low_half(("h", t, g))
                        if t == 2:
                            low(29)
                    dve.wait_ge(squares, 30)
                    chain.link(rsqrt(dve, chain, MS[:, 25:30], RS[:, 25:30], 5))
                    nc.vector.tensor_scalar(HR[:, 0:5], RS[:, 25:30], 0.5, None, ALU.mult).then_inc(rstd_ready, 1)
                    for i in range(30, 33):
                        low(i)
                    for half in range(2):
                        for t in range(TILES):
                            emb = EMB[half][t]
                            gate(emb, emb, acc_drained[t], BLK["pg0"] + half + 1).then_inc(gated, 1)
                            if half == 0 and t == 1:
                                low(33)
                            dve.wait_ge(gated, (5 + half) * TILES + t + 1)
                            hh = H[:, t, 512 * half:512 * (half + 1)]
                            stt(out=hh, in0=emb, scalar=0.5, in1=hh, op0=ALU.mult, op1=ALU.add).then_inc(h_done, 1)
                        if half == 0:
                            low(34)
                            low(35)

                @block.gpsimd
                def _(pool):
                    for s in range(CACHED):
                        load_cache(pool, layer, s, cache_in[s])
                    pool.dma_start(a["new_conv_sample"][bass.ds(layer, 1), :, 0:STATE - NS, :],
                                   a["state_conv"][bass.ds(layer, 1), :, NS:STATE, :]).then_inc(states_stored, 16)
                    pool.wait_ge(latents_ready, 1)
                    for name, rows, col, n in (("new_ckv", None, QLORA, LORA), ("new_krope", None, NZ - ROPE, ROPE)):
                        pool.dma_start(at(name + "_prompt").rearrange("l o (t p) r -> p (l o t) r", p=P),
                                       Z[:, 0:4, col:col + n]).then_inc(latents_stored, 16)
                        pool.dma_start(at(name + "_sample").rearrange("o b s r -> (o b s) r"),
                                       Z[:, 4, col:col + n]).then_inc(latents_stored, 16)
                    pool.wait_ge(gated, 2 * TILES)
                    pool.dma_start(at("new_conv_prompt").rearrange("l o s c -> (l o s) c"),
                                   Y[P - STATE:P, TILES - 2, 512:1024]).then_inc(u_stored, 16)
                    for s in range(NB):
                        pool.dma_start(a["new_conv_sample"][bass.ds(layer, 1), s, STATE - NS:STATE, :].rearrange("o s c -> (o s) c"),
                                       Y[NS * s:NS * (s + 1), TILES - 1, 512:1024]).then_inc(u_stored, 16)
                    for s in range(CACHED, NB):
                        filled_wait(pool, ("o", s - CACHED))
                        load_cache(pool, layer, s, cache_in[s % CACHED])
                    filled_wait(pool, ("o", NB - 1))
                    pool.dma_start(LCG, at("ln_conv_g").to_broadcast([P, CH])).then_inc(lnconv_in, 16)
                    pool.dma_start(LCB, at("ln_conv_b").to_broadcast([P, CH])).then_inc(lnconv_in, 16)
                    pool.wait_ge(lnconv_in, 32)
                    for t in range(TILES):
                        pool.wait_ge(ln_scaled, t + 1)
                        v = VT[:, 512 * t:512 * (t + 1)]
                        nc.gpsimd.tensor_tensor(v, v, LCB, ALU.add).then_inc(ln_done, 1)
                    pool.wait_ge(latents_stored, 64)
                    pool.wait_ge(u_stored, 16 * (1 + NB))
                    pool.wait_ge(states_stored, 16)

            nc.gpsimd.dma_reset(range(sems[0].num, sems[-1].num + 1))
            nc.gpsimd.sem_clear(range(sems[0].num, sems[-1].num + 1))
            nc.all_engine_barrier()

        LNF = WR[:, 0, :, :].rearrange("p k n -> p (k n)")
        with nc.Block() as block:
            @block.sync
            def _(sp):
                sp.dma_start(LNF, a["ln_f"].unsqueeze(0).to_broadcast([P, D])).then_inc(final_in, 16)
                for t in range(TILES):
                    sp.wait_ge(h_done, t + 1)
                    dst = a["y_prompt"][0, P * t:P * (t + 1), :] if t < 4 else a["y_sample"].rearrange("b s d -> (b s) d")
                    sp.dma_start(dst, H[:, t, :]).then_inc(y_stored, 16)
                sp.wait_ge(y_stored, 16 * TILES)

            @block.scalar
            def _(act):
                for t in range(TILES):
                    if t:
                        act.wait_ge(squares, t)
                    nc.scalar.activation(JUNK[:, :], H[:, t, :], ACT.Square, scale=D ** -0.5,
                                         accum_out=MS[:, t:t + 1]).then_inc(squares, 1)

            @block.vector
            def _(dve):
                chain = Chain(dve, dve_chain)
                dve.wait_ge(squares, TILES)
                chain.link(rsqrt(dve, chain, MS[:, 0:5], RS[:, 0:5], 5))
                dve.wait_ge(final_in, 16)
                for t in range(TILES):
                    nc.vector.scalar_tensor_tensor(out=H[:, t, :], in0=H[:, t, :], scalar=RS[:, t:t + 1], in1=LNF,
                                                   op0=ALU.mult, op1=ALU.mult).then_inc(h_done, 1)


_INS = ["x_prompt", "x_sample", "cache_ckv", "cache_krope", "state_conv", "p_prompt", "p_sample", "ln_in", "w_in",
        "ln_q", "w_q_b", "ln_kv", "w_kv_b", "conv_w", "conv_b", "ln_conv_g", "ln_conv_b", "ln_out_a", "ln_out_c",
        "w_out", "w_pe", "ln_pg", "w_pg", "ln_f"]
_OUTS = [("y_prompt", (1, SEQ, D)), ("y_sample", (NB, NS, D)),
         ("new_ckv_prompt", (DEPTH, 1, SEQ, LORA)), ("new_krope_prompt", (DEPTH, 1, SEQ, ROPE)),
         ("new_conv_prompt", (DEPTH, 1, STATE, CH)),
         ("new_ckv_sample", (DEPTH, NB, NS, LORA)), ("new_krope_sample", (DEPTH, NB, NS, ROPE)),
         ("new_conv_sample", (DEPTH, NB, STATE, CH))]


def constants():
    import numpy as np
    f = np.float32
    half = ROPE // 2
    inv = (f(10000.0) ** (-np.arange(half, dtype=f) / f(half))).astype(f)
    pos = np.concatenate([np.arange(SEQ), np.tile(PAST + np.arange(NS), NB)]).astype(f)
    ang = pos[:, None] * inv[None, :]
    cos, sin = np.cos(ang).astype(f), np.sin(ang).astype(f)
    ropet = np.ones((P, TOK), f)
    ropet[64:80] = cos.T
    ropet[80:96] = cos.T
    ropet[96:112] = -sin.T
    ropet[112:128] = sin.T
    ropek = np.stack([cos, cos, -sin, sin], axis=1).reshape(TILES, P, 4, half).transpose(1, 0, 2, 3)
    mrow = np.full((1, 240), NEG, f)
    mrow[0, 112:128] = 0.0
    return {"c_ident": np.eye(P, dtype=f), "c_ropet": ropet, "c_ropek": np.ascontiguousarray(ropek), "c_mrow": mrow}


def kernel(**inputs):
    import numpy as _np
    import concourse.bacc as _bacc
    from concourse import mybir as _mybir
    from concourse.bass_utils import run_bass_kernel_spmd as _run

    nc = _bacc.Bacc("TRN2", target_bir_lowering=False, num_devices=1)
    given = {name: _np.ascontiguousarray(inputs[name]) for name in _INS}
    given.update(constants())
    arrays, aps = {}, {}
    for name, x in given.items():
        arrays[f"in_{name}_dram"] = x
        aps[name] = nc.dram_tensor(f"in_{name}_dram", x.shape, _mybir.dt.from_np(x.dtype), kind="ExternalInput").ap()
    for name, shape in _OUTS:
        aps[name] = nc.dram_tensor(f"out_{name}_dram", shape, F32, kind="ExternalOutput").ap()
    build(nc, aps)
    r = _run(nc, [arrays], core_ids=[0])
    return tuple(r.results[0][f"out_{name}_dram"] for name, _ in _OUTS)
```
